# Optimizing a Trainium2 kernel written in Bass

```python
import math
import jax
import jax.numpy as jnp
from jax import lax
import numpy as np

D_MODEL = 1024
BATCH = 1
SEQ = 256
DEPTH = 2

GRID_W = 64
CTX_LEN = 256
ROPE_BASE = 10000.0
NORM_EPS = 1e-6
Q_BLOCK = 128

MLA_HEADS = 8
MLA_Q_LORA = 256
MLA_KV_LORA = 128
MLA_NOPE = 64
MLA_ROPE = 32
MLA_V = 64
MLA_SCALE = (MLA_NOPE + MLA_ROPE) ** -0.5

GQA_HEADS = 8
GQA_KV_HEADS = 2
GQA_DIM = 64
GQA_SCALE = GQA_DIM ** -0.5

SSD_HEADS = 8
SSD_HEAD_DIM = 64
SSD_INNER = SSD_HEADS * SSD_HEAD_DIM
SSD_GROUPS = 2
SSD_STATE = 128
SSD_CONV = 3
SSD_CHUNK = 128
SSD_XBC = SSD_INNER + 2 * SSD_GROUPS * SSD_STATE

DIFF_HEADS = 4
DIFF_DIM = 64
DIFF_V = 2 * DIFF_DIM
DIFF_SCALE = DIFF_DIM ** -0.5

N_EXPERTS = 64
TOP_K = 8
N_GROUPS = 8
TOPK_GROUPS = 4
EXPERT_FF = 256
SHARED_FF = 256
ROUTED_SCALE = 2.5
MOE_BLOCK = 128

ATT_SPLITS = (MLA_Q_LORA, MLA_KV_LORA, MLA_ROPE, GQA_HEADS * GQA_DIM, GQA_KV_HEADS * GQA_DIM, GQA_KV_HEADS * GQA_DIM)
REC_SPLITS = (SSD_INNER, SSD_XBC, SSD_HEADS, SSD_HEADS, 2 * DIFF_HEADS * DIFF_DIM, 2 * DIFF_HEADS * DIFF_DIM, DIFF_HEADS * DIFF_V)
ATT_IN = sum(ATT_SPLITS)
REC_IN = sum(REC_SPLITS)
MIX_WIDTH = MLA_HEADS * MLA_V + GQA_HEADS * GQA_DIM
N_EVEN = (DEPTH + 1) // 2
N_ODD = DEPTH // 2

kernel_name = 'hybrid_dit_mla_gqa_ssd_diffattn_moe'

def rms_norm(x, g):
    xf = x.astype(jnp.float32)
    y = xf * lax.rsqrt(jnp.mean(xf * xf, axis=-1, keepdims=True) + NORM_EPS)
    return (y * g.astype(jnp.float32)).astype(x.dtype)

def _split(p, sizes):
    return jnp.split(p, [int(s) for s in np.cumsum(sizes)[:-1]], axis=-1)

def axial_rope_tables(n_tokens, dim):
    rows = n_tokens // GRID_W
    row = jnp.repeat(jnp.arange(rows, dtype=jnp.float32), GRID_W)
    col = jnp.tile(jnp.arange(GRID_W, dtype=jnp.float32), rows)
    half = dim // 2
    inv = ROPE_BASE ** (-(jnp.arange(half // 2, dtype=jnp.float32) * 2.0 / half))
    ang_r = row[:, None] * inv
    ang_c = col[:, None] * inv
    ang = jnp.concatenate([ang_r, ang_r, ang_c, ang_c], axis=-1)
    return jnp.cos(ang), jnp.sin(ang)

def apply_rope(x, cos, sin):
    half = x.shape[-1] // 2
    def rot(u):
        u1, u2 = jnp.split(u, 2, axis=-1)
        return jnp.concatenate([-u2, u1], axis=-1)
    rotated = jnp.concatenate([rot(x[..., :half]), rot(x[..., half:])], axis=-1)
    cos = cos[None, :, None, :].astype(x.dtype)
    sin = sin[None, :, None, :].astype(x.dtype)
    return x * cos + rotated * sin

def block_attention(q, k, v, scale):
    b, nq, h, dk = q.shape
    hk, dv = k.shape[2], v.shape[-1]
    g = h // hk
    nb = nq // Q_BLOCK
    qb = jnp.moveaxis(q.reshape(b, nb, Q_BLOCK, hk, g, dk), 1, 0)
    def one_block(qi):
        s = jnp.einsum('bqkgd,bskd->bkgqs', qi, k).astype(jnp.float32) * scale
        p = jax.nn.softmax(s, axis=-1).astype(v.dtype)
        return jnp.einsum('bkgqs,bskd->bqkgd', p, v)
    o = lax.map(one_block, qb)
    return jnp.moveaxis(o, 0, 1).reshape(b, nq, h, dv)

def block_diff_attention(q, k, v, lam, scale):
    b, nq, h, _, d = q.shape
    dv = v.shape[-1]
    nb = nq // Q_BLOCK
    qb = jnp.moveaxis(q.reshape(b, nb, Q_BLOCK, h, 2, d), 1, 0)
    def one_block(qi):
        s = jnp.einsum('bqhmd,bshmd->bmhqs', qi, k).astype(jnp.float32) * scale
        p = jax.nn.softmax(s, axis=-1)
        w = (p[:, 0] - lam * p[:, 1]).astype(v.dtype)
        return jnp.einsum('bhqs,bshe->bqhe', w, v)
    o = lax.map(one_block, qb)
    return jnp.moveaxis(o, 0, 1).reshape(b, nq, h, dv)

def attn_project(hh, w_in, q_norm, w_q_up, kv_norm, w_kv_up, gqa_qn, gqa_kn, rope_mla, rope_hd):
    b, n, _ = hh.shape
    q_lat, kv_lat, k_pe, gq, gk, gv = _split(hh @ w_in, ATT_SPLITS)
    q = (rms_norm(q_lat, q_norm) @ w_q_up).reshape(b, n, MLA_HEADS, MLA_NOPE + MLA_ROPE)
    kv = (rms_norm(kv_lat, kv_norm) @ w_kv_up).reshape(b, n, MLA_HEADS, MLA_NOPE + MLA_V)
    q_nope, q_pe = q[..., :MLA_NOPE], q[..., MLA_NOPE:]
    k_nope, v_mla = kv[..., :MLA_NOPE], kv[..., MLA_NOPE:]
    k_pe = k_pe[:, :, None, :]
    gq = rms_norm(gq.reshape(b, n, GQA_HEADS, GQA_DIM), gqa_qn)
    gk = rms_norm(gk.reshape(b, n, GQA_KV_HEADS, GQA_DIM), gqa_kn)
    gv = gv.reshape(b, n, GQA_KV_HEADS, GQA_DIM)
    if rope_mla is not None:
        q_pe = apply_rope(q_pe, *rope_mla)
        k_pe = apply_rope(k_pe, *rope_mla)
        gq = apply_rope(gq, *rope_hd)
        gk = apply_rope(gk, *rope_hd)
    q_mla = jnp.concatenate([q_nope, q_pe], axis=-1)
    k_mla = jnp.concatenate([k_nope, jnp.broadcast_to(k_pe, (b, n, MLA_HEADS, MLA_ROPE))], axis=-1)
    return (q_mla, k_mla, v_mla), (gq, gk, gv)

def attn_mixer(u, uc, w_in, q_norm, w_q_up, kv_norm, w_kv_up, gqa_qn, gqa_kn, w_out, rope_mla, rope_hd, need_ctx):
    (qa, ka, va), (qb, kb, vb) = attn_project(u, w_in, q_norm, w_q_up, kv_norm, w_kv_up, gqa_qn, gqa_kn, rope_mla, rope_hd)
    (qac, kac, vac), (qbc, kbc, vbc) = attn_project(uc, w_in, q_norm, w_q_up, kv_norm, w_kv_up, gqa_qn, gqa_kn, None, None)
    cat = lambda a, a_c: jnp.concatenate([a, a_c], axis=1)
    def merge(oa, ob):
        return jnp.concatenate([oa.reshape(*oa.shape[:2], -1), ob.reshape(*ob.shape[:2], -1)], axis=-1) @ w_out
    out = merge(block_attention(qa, cat(ka, kac), cat(va, vac), MLA_SCALE),
                block_attention(qb, cat(kb, kbc), cat(vb, vbc), GQA_SCALE))
    out_c = None
    if need_ctx:
        out_c = merge(block_attention(qac, kac, vac, MLA_SCALE), block_attention(qbc, kbc, vbc, GQA_SCALE))
    return out, out_c

def centred_dwconv(u, w, bias):
    k = w.shape[0]
    out = lax.conv_general_dilated(u, w[:, None, :], window_strides=(1,), padding=[(k // 2, k // 2)],
                                   dimension_numbers=('NWC', 'WIO', 'NWC'), feature_group_count=u.shape[-1])
    return out + bias

def ssd_scan(x, dt, a, bm, cm, init_state, want_y):
    b, l, h, p = x.shape
    g, n = bm.shape[2], bm.shape[3]
    hg = h // g
    nc = l // SSD_CHUNK
    xs = (x * dt[..., None].astype(x.dtype)).reshape(b, nc, SSD_CHUNK, g, hg, p)
    adt = (dt * a).reshape(b, nc, SSD_CHUNK, g, hg)
    a_cs = jnp.cumsum(jnp.moveaxis(adt, 2, -1), axis=-1)
    bc = bm.reshape(b, nc, SSD_CHUNK, g, n)
    cc = cm.reshape(b, nc, SSD_CHUNK, g, n)
    decay_to_end = jnp.exp(a_cs[..., -1:] - a_cs)
    chunk_states = jnp.einsum('bcsgn,bcghs,bcsghp->bcghpn', bc, decay_to_end, xs)
    chunk_decay = jnp.exp(a_cs[..., -1])
    def step(state, inp):
        dec, st = inp
        return state * dec[..., None, None] + st, state
    final, prev = lax.scan(step, init_state, (jnp.moveaxis(chunk_decay, 1, 0), jnp.moveaxis(chunk_states, 1, 0)))
    if not want_y:
        return None, final
    prev = jnp.moveaxis(prev, 0, 1)
    seg = a_cs[..., :, None] - a_cs[..., None, :]
    lower = jnp.tril(jnp.ones((SSD_CHUNK, SSD_CHUNK), dtype=bool))
    lmat = jnp.exp(jnp.where(lower, seg, -jnp.inf))
    cb = jnp.einsum('bclgn,bcsgn->bcgls', cc, bc)
    y_diag = jnp.einsum('bcgls,bcghls,bcsghp->bclghp', cb, lmat, xs)
    y_off = jnp.einsum('bclgn,bcghpn,bcghl->bclghp', cc, prev, jnp.exp(a_cs))
    y = (y_diag + y_off).reshape(b, l, h, p)
    return y.astype(x.dtype), final

def ssd_direction(lat, ctxs, dt_bias, a_log, reverse, need_ctx):
    a = -jnp.exp(a_log.astype(jnp.float32))
    def prep(xs, bm, cm, dt_raw):
        dt = jax.nn.softplus(dt_raw.astype(jnp.float32) + dt_bias.astype(jnp.float32))
        seq = (xs, bm, cm, dt)
        if reverse:
            seq = tuple(jnp.flip(t, axis=1) for t in seq)
        return seq
    xl, bl, cl, dtl = prep(*lat)
    xc, bcx, ccx, dtc = prep(*ctxs)
    init = jnp.zeros((xl.shape[0], SSD_GROUPS, SSD_HEADS // SSD_GROUPS, SSD_HEAD_DIM, SSD_STATE), jnp.float32)
    yc, state_c = ssd_scan(xc, dtc, a, bcx, ccx, init, need_ctx)
    yl, _ = ssd_scan(xl, dtl, a, bl, cl, state_c, True)
    if reverse:
        yl = jnp.flip(yl, axis=1)
        yc = jnp.flip(yc, axis=1) if yc is not None else None
    return yl, yc

def rec_project(hh, w_in, conv_w, conv_b, rope_hd):
    b, n, _ = hh.shape
    z, xbc, dt_f, dt_b, dq, dk, dv = _split(hh @ w_in, REC_SPLITS)
    xbc = jax.nn.silu(centred_dwconv(xbc, conv_w, conv_b))
    xs, bm, cm = _split(xbc, (SSD_INNER, SSD_GROUPS * SSD_STATE, SSD_GROUPS * SSD_STATE))
    xs = xs.reshape(b, n, SSD_HEADS, SSD_HEAD_DIM)
    bm = bm.reshape(b, n, SSD_GROUPS, SSD_STATE)
    cm = cm.reshape(b, n, SSD_GROUPS, SSD_STATE)
    dq = dq.reshape(b, n, 2 * DIFF_HEADS, DIFF_DIM)
    dk = dk.reshape(b, n, 2 * DIFF_HEADS, DIFF_DIM)
    if rope_hd is not None:
        dq = apply_rope(dq, *rope_hd)
        dk = apply_rope(dk, *rope_hd)
    dq = dq.reshape(b, n, DIFF_HEADS, 2, DIFF_DIM)
    dk = dk.reshape(b, n, DIFF_HEADS, 2, DIFF_DIM)
    dv = dv.reshape(b, n, DIFF_HEADS, DIFF_V)
    return (z, xs, bm, cm, dt_f, dt_b), (dq, dk, dv)

def rec_mixer(u, uc, w_in, conv_w, conv_b, dt_bias_f, dt_bias_b, a_log_f, a_log_b, d_skip, ssd_norm,
              lq1, lk1, lq2, lk2, subln, w_out, lambda_init, rope_hd, need_ctx):
    (z, xs, bm, cm, dtf, dtb), (dq, dk, dv) = rec_project(u, w_in, conv_w, conv_b, rope_hd)
    (zc, xsc, bmc, cmc, dtfc, dtbc), (dqc, dkc, dvc) = rec_project(uc, w_in, conv_w, conv_b, None)
    yf, yfc = ssd_direction((xs, bm, cm, dtf), (xsc, bmc, cmc, dtfc), dt_bias_f, a_log_f, False, need_ctx)
    yb, ybc = ssd_direction((xs, bm, cm, dtb), (xsc, bmc, cmc, dtbc), dt_bias_b, a_log_b, True, need_ctx)
    f32 = jnp.float32
    lam = (jnp.exp(jnp.sum(lq1.astype(f32) * lk1.astype(f32))) - jnp.exp(jnp.sum(lq2.astype(f32) * lk2.astype(f32)))
           + lambda_init)
    def ssd_out(y_f, y_b, x_in, zz):
        b, n = zz.shape[:2]
        y = (y_f + y_b + x_in * d_skip[:, None]).reshape(b, n, SSD_INNER) * jax.nn.silu(zz)
        y = rms_norm(y.reshape(b, n, SSD_GROUPS, -1), ssd_norm.reshape(SSD_GROUPS, -1))
        return y.reshape(b, n, SSD_INNER)
    def diff_out(o):
        b, n = o.shape[:2]
        return (rms_norm(o, subln) * (1.0 - lambda_init)).reshape(b, n, DIFF_HEADS * DIFF_V)
    cat = lambda a, a_c: jnp.concatenate([a, a_c], axis=1)
    o_d = block_diff_attention(dq, cat(dk, dkc), cat(dv, dvc), lam, DIFF_SCALE)
    out = jnp.concatenate([ssd_out(yf, yb, xs, z), diff_out(o_d)], axis=-1) @ w_out
    out_c = None
    if need_ctx:
        o_dc = block_diff_attention(dqc, dkc, dvc, lam, DIFF_SCALE)
        out_c = jnp.concatenate([ssd_out(yfc, ybc, xsc, zc), diff_out(o_dc)], axis=-1) @ w_out
    return out, out_c

def moe_ffn(t, router_w, router_b, w_gate, w_up, w_down, sh_gate, sh_up, sh_down):
    n_tok, d = t.shape
    scores = jax.nn.sigmoid((t @ router_w).astype(jnp.float32))
    sel = scores + router_b.astype(jnp.float32)
    grp_score = jnp.sum(lax.top_k(sel.reshape(n_tok, N_GROUPS, -1), 2)[0], axis=-1)
    _, grp_idx = lax.top_k(grp_score, TOPK_GROUPS)
    grp_mask = jnp.sum(jax.nn.one_hot(grp_idx, N_GROUPS, dtype=jnp.float32), axis=1) > 0
    masked = jnp.where(jnp.repeat(grp_mask, N_EXPERTS // N_GROUPS, axis=-1), sel, -jnp.inf)
    _, top_idx = lax.top_k(masked, TOP_K)
    top_w = jnp.take_along_axis(scores, top_idx, axis=-1)
    top_w = top_w / jnp.sum(top_w, axis=-1, keepdims=True) * ROUTED_SCALE
    n_asg = n_tok * TOP_K
    flat_e = top_idx.reshape(-1)
    flat_tok = jnp.arange(n_asg, dtype=jnp.int32) // TOP_K
    flat_w = top_w.reshape(-1)
    order = jnp.argsort(flat_e)
    e_sorted = flat_e[order]
    counts = jnp.bincount(flat_e, length=N_EXPERTS)
    padded = (counts + MOE_BLOCK - 1) // MOE_BLOCK * MOE_BLOCK
    pad_end = jnp.cumsum(padded)
    pad_start = pad_end - padded
    start = jnp.cumsum(counts) - counts
    dest = pad_start[e_sorted] + jnp.arange(n_asg, dtype=jnp.int32) - start[e_sorted]
    n_blocks = -(-n_asg // MOE_BLOCK) + N_EXPERTS
    slot_tok = jnp.zeros((n_blocks * MOE_BLOCK,), jnp.int32).at[dest].set(flat_tok[order])
    slot_w = jnp.zeros((n_blocks * MOE_BLOCK,), jnp.float32).at[dest].set(flat_w[order])
    block_exp = jnp.minimum(jnp.searchsorted(pad_end, jnp.arange(n_blocks) * MOE_BLOCK, side='right'), N_EXPERTS - 1)
    shared = (jax.nn.silu(t @ sh_gate) * (t @ sh_up)) @ sh_down
    def body(acc, blk):
        e, tok, w = blk
        xb = t[tok]
        hid = jax.nn.silu(xb @ w_gate[e]) * (xb @ w_up[e])
        yb = (hid @ w_down[e]) * w[:, None].astype(t.dtype)
        return acc.at[tok].add(yb), None
    out, _ = lax.scan(body, shared, (block_exp, slot_tok.reshape(n_blocks, MOE_BLOCK), slot_w.reshape(n_blocks, MOE_BLOCK)))
    return out

def setup_inputs(seed: int = 0) -> dict:
    key = jax.random.key(seed)
    ks = iter(jax.random.split(key, 64))
    f32 = jnp.float32
    def nrm(shape, fan_in, scale=1.0):
        return jax.random.normal(next(ks), shape, f32) * (scale * fan_in ** -0.5)
    def gain(shape):
        return 1.0 + 0.02 * jax.random.normal(next(ks), shape, f32)
    def small(shape, s):
        return s * jax.random.normal(next(ks), shape, f32)
    def dt_bias(shape):
        u = jax.random.uniform(next(ks), shape, f32, minval=math.log(1e-3), maxval=math.log(1e-1))
        dt = jnp.exp(u)
        return dt + jnp.log(-jnp.expm1(-dt))
    def a_log(shape):
        return jnp.log(jax.random.uniform(next(ks), shape, f32, minval=1.0, maxval=16.0))
    D = D_MODEL
    return {
        'x': jax.random.normal(next(ks), (BATCH, SEQ, D), f32),
        'c': jax.random.normal(next(ks), (BATCH, D), f32),
        'ctx': jax.random.normal(next(ks), (BATCH, CTX_LEN, D), f32),
        'c_ctx': jax.random.normal(next(ks), (D,), f32),
        'ada_w': nrm((DEPTH, D, 6 * D), D, 0.5),
        'ada_b': small((DEPTH, 6 * D), 0.02),
        'norm_mix_pre': gain((DEPTH, D)),
        'norm_mix_post': gain((DEPTH, D)),
        'norm_ffn_pre': gain((DEPTH, D)),
        'norm_ffn_post': gain((DEPTH, D)),
        'mix_w_out': nrm((DEPTH, MIX_WIDTH, D), MIX_WIDTH),
        'att_w_in': nrm((N_EVEN, D, ATT_IN), D),
        'mla_q_norm': gain((N_EVEN, MLA_Q_LORA)),
        'mla_w_q_up': nrm((N_EVEN, MLA_Q_LORA, MLA_HEADS * (MLA_NOPE + MLA_ROPE)), MLA_Q_LORA),
        'mla_kv_norm': gain((N_EVEN, MLA_KV_LORA)),
        'mla_w_kv_up': nrm((N_EVEN, MLA_KV_LORA, MLA_HEADS * (MLA_NOPE + MLA_V)), MLA_KV_LORA),
        'gqa_q_norm': gain((N_EVEN, GQA_DIM)),
        'gqa_k_norm': gain((N_EVEN, GQA_DIM)),
        'rec_w_in': nrm((N_ODD, D, REC_IN), D),
        'ssd_conv_w': nrm((N_ODD, SSD_CONV, SSD_XBC), SSD_CONV),
        'ssd_conv_b': small((N_ODD, SSD_XBC), 0.02),
        'ssd_dt_bias_f': dt_bias((N_ODD, SSD_HEADS)),
        'ssd_dt_bias_b': dt_bias((N_ODD, SSD_HEADS)),
        'ssd_a_log_f': a_log((N_ODD, SSD_HEADS)),
        'ssd_a_log_b': a_log((N_ODD, SSD_HEADS)),
        'ssd_d': gain((N_ODD, SSD_HEADS)),
        'ssd_norm': gain((N_ODD, SSD_INNER)),
        'diff_lambda_q1': small((N_ODD, DIFF_DIM), 0.1),
        'diff_lambda_k1': small((N_ODD, DIFF_DIM), 0.1),
        'diff_lambda_q2': small((N_ODD, DIFF_DIM), 0.1),
        'diff_lambda_k2': small((N_ODD, DIFF_DIM), 0.1),
        'diff_subln': gain((N_ODD, DIFF_V)),
        'router_w': nrm((DEPTH, D, N_EXPERTS), D),
        'router_b': small((DEPTH, N_EXPERTS), 0.01),
        'exp_w_gate': nrm((DEPTH, N_EXPERTS, D, EXPERT_FF), D),
        'exp_w_up': nrm((DEPTH, N_EXPERTS, D, EXPERT_FF), D),
        'exp_w_down': nrm((DEPTH, N_EXPERTS, EXPERT_FF, D), EXPERT_FF),
        'sh_w_gate': nrm((DEPTH, D, SHARED_FF), D),
        'sh_w_up': nrm((DEPTH, D, SHARED_FF), D),
        'sh_w_down': nrm((DEPTH, SHARED_FF, D), SHARED_FF),
    }

def reference(x, c, ctx, c_ctx, ada_w, ada_b, norm_mix_pre, norm_mix_post, norm_ffn_pre, norm_ffn_post, mix_w_out,
              att_w_in, mla_q_norm, mla_w_q_up, mla_kv_norm, mla_w_kv_up, gqa_q_norm, gqa_k_norm,
              rec_w_in, ssd_conv_w, ssd_conv_b, ssd_dt_bias_f, ssd_dt_bias_b, ssd_a_log_f, ssd_a_log_b, ssd_d, ssd_norm,
              diff_lambda_q1, diff_lambda_k1, diff_lambda_q2, diff_lambda_k2, diff_subln,
              router_w, router_b, exp_w_gate, exp_w_up, exp_w_down, sh_w_gate, sh_w_up, sh_w_down):
    b, n, d = x.shape
    n_ctx = ctx.shape[1]
    rope_mla = axial_rope_tables(n, MLA_ROPE)
    rope_hd = axial_rope_tables(n, GQA_DIM)
    silu_c = jax.nn.silu(c)
    silu_cc = jax.nn.silu(c_ctx)
    h, hc = x, ctx
    for i in range(DEPTH):
        last = i == DEPTH - 1
        j = i // 2
        shift1, scale1, gate1, shift2, scale2, gate2 = jnp.split((silu_c @ ada_w[i] + ada_b[i])[:, None, :], 6, axis=-1)
        shift1c, scale1c, gate1c, shift2c, scale2c, gate2c = jnp.split((silu_cc @ ada_w[i] + ada_b[i])[None, None, :], 6, axis=-1)
        u = rms_norm(h, norm_mix_pre[i]) * (1 + scale1) + shift1
        uc = rms_norm(hc, norm_mix_pre[i]) * (1 + scale1c) + shift1c
        if i % 2 == 0:
            o, oc = attn_mixer(u, uc, att_w_in[j], mla_q_norm[j], mla_w_q_up[j], mla_kv_norm[j], mla_w_kv_up[j],
                               gqa_q_norm[j], gqa_k_norm[j], mix_w_out[i], rope_mla, rope_hd, not last)
        else:
            lambda_init = 0.8 - 0.6 * math.exp(-0.3 * i)
            o, oc = rec_mixer(u, uc, rec_w_in[j], ssd_conv_w[j], ssd_conv_b[j], ssd_dt_bias_f[j], ssd_dt_bias_b[j],
                              ssd_a_log_f[j], ssd_a_log_b[j], ssd_d[j], ssd_norm[j],
                              diff_lambda_q1[j], diff_lambda_k1[j], diff_lambda_q2[j], diff_lambda_k2[j], diff_subln[j],
                              mix_w_out[i], lambda_init, rope_hd, not last)
        h = h + gate1 * rms_norm(o, norm_mix_post[i])
        v = rms_norm(h, norm_ffn_pre[i]) * (1 + scale2) + shift2
        if last:
            f = moe_ffn(v.reshape(b * n, d), router_w[i], router_b[i], exp_w_gate[i], exp_w_up[i], exp_w_down[i],
                        sh_w_gate[i], sh_w_up[i], sh_w_down[i]).reshape(b, n, d)
        else:
            hc = hc + gate1c * rms_norm(oc, norm_mix_post[i])
            vc = rms_norm(hc, norm_ffn_pre[i]) * (1 + scale2c) + shift2c
            f_all = moe_ffn(jnp.concatenate([v.reshape(b * n, d), vc.reshape(b * n_ctx, d)], axis=0),
                            router_w[i], router_b[i], exp_w_gate[i], exp_w_up[i], exp_w_down[i],
                            sh_w_gate[i], sh_w_up[i], sh_w_down[i])
            f = f_all[:b * n].reshape(b, n, d)
            hc = hc + gate2c * rms_norm(f_all[b * n:].reshape(b, n_ctx, d), norm_ffn_post[i])
        h = h + gate2 * rms_norm(f, norm_ffn_post[i])
    return h


_drawn_inputs = setup_inputs


def setup_inputs(seed=0):
    import zlib

    import numpy as np

    out = dict(_drawn_inputs(seed))
    spreads = {}
    factors = {'norm_mix_pre': 2.812,
     'norm_ffn_post': 3.964,
     'mla_q_norm': 3.424,
     'mla_kv_norm': 2.859,
     'gqa_q_norm': 4.959,
     'gqa_k_norm': 5.766,
     'ssd_conv_b': 12.845,
     'ssd_d': 200.0,
     'ssd_norm': 24.208,
     'diff_lambda_k2': 80.382,
     'diff_subln': 20.94}
    for name, (base, spread) in spreads.items():
        noise = np.random.default_rng([zlib.crc32(name.encode()), seed]).standard_normal(out[name].shape)
        drawn = base * np.exp(spread * noise) if base else spread * noise
        out[name] = jnp.asarray(drawn.astype(out[name].dtype))
    for name, factor in factors.items():
        out[name] = (out[name] * factor).astype(out[name].dtype)
    return out
```

```python
import math
from contextlib import ExitStack

import numpy as np

import concourse.bass as bass
from concourse import mybir

F32 = mybir.dt.float32
BF16 = mybir.dt.bfloat16
I32 = mybir.dt.int32
ACT = mybir.ActivationFunctionType
ALU = mybir.AluOpType
AX = mybir.AxisListType.X

P = 128
D = 1024
KC = D // P
SEQ, CTX = 256, 256
NT = (SEQ + CTX) // P
NL = SEQ // P
EPS = 1e-6
MH, NOPE, ROPE, MV = 8, 64, 32, 64
QK = NOPE + ROPE
QLORA, KVLORA = 256, 128
GH, GKV, GD = 8, 2, 64
ATT_IN = QLORA + KVLORA + ROPE + (GH + 2 * GKV) * GD
C_KV, C_PE, C_GQ = QLORA, QLORA + KVLORA, QLORA + KVLORA + ROPE
C_GK = C_GQ + GH * GD
C_GV = C_GK + GKV * GD
SH, SP_, SG, SN = 8, 64, 2, 128
SI = SH * SP_
XBC = SI + 2 * SG * SN
DH, DD, DV = 4, 64, 128
R_XBC, R_DT = SI, SI + XBC
R_DQ = R_DT + 2 * SH
R_DK, R_DV = R_DQ + 2 * DH * DD, R_DQ + 4 * DH * DD
NE, TOPK, NG, TG = 64, 8, 8, 4
FF = 256
ROUTED_SCALE = 2.5
BLOCKS = (SEQ + CTX) * TOPK // P + NE
NEG = -1.0e30
GONE = -3.0e38
WSLOT = KC * 512
WSLOTS = 3
UNROLL = 4
AHEAD = UNROLL + 1
FAR = 32768.0

CONST = {}


def const_table():
    i = np.arange(P)
    cols = {
        "ident": np.eye(P),
        "tri_le": i[:, None] <= i[None, :],
        "tri_ge": i[:, None] >= i[None, :],
        "tri_lt": i[:, None] < i[None, :],
        "ones": np.ones((P, P)),
        "iota": np.broadcast_to(i[None, :], (P, P)),
        "spot": np.broadcast_to(np.stack([i, 0 * i, 0 * i + 1], 1)[:, None, :] + np.arange(NT)[None, :, None] * np.array([0, 1, 0]), (P, NT, 3)).reshape(P, -1),
        "spot_words": np.broadcast_to(np.array([[1, P, -FAR, 0], [TOPK, TOPK * P, -FAR, 1]]).reshape(1, -1), (P, 8)),
        "base": np.broadcast_to(np.arange(BLOCKS + 8)[None, :], (P, BLOCKS + 8)),
        "lower": np.broadcast_to((np.arange(NG)[None, :] < np.arange(NG)[:, None]).reshape(1, -1), (P, NG * NG)),
        "eps": np.full((P, 1), EPS),
        "one": np.ones((P, 1)),
    }
    for dim in (ROPE, GD):
        half = dim // 2
        inv = (np.float32(10000.0) ** (-(np.arange(half // 2, dtype=np.float32) * np.float32(2.0) / half))).astype(np.float32)
        row = np.repeat(np.arange(SEQ // 64, dtype=np.float32), 64)
        col = np.tile(np.arange(64, dtype=np.float32), SEQ // 64)
        ar, ac = row[:, None] * inv, col[:, None] * inv
        ang = np.concatenate([ar, ar, ac, ac], axis=-1).astype(np.float32)
        sign = np.tile(np.repeat([-1.0, 1.0], half // 2), 2)
        for name, v in (("cos", np.cos(ang)), ("sin", np.sin(ang) * sign)):
            cols[f"{name}{dim}"] = v.reshape(NL, P, dim).transpose(1, 0, 2).reshape(P, NL * dim)
    at = 0
    for name, v in cols.items():
        CONST[name] = (at, v.shape[1])
        at += v.shape[1]
    return np.ascontiguousarray(np.concatenate([v.astype(np.float32) for v in cols.values()], axis=1))


class Chain:

    def __init__(self, eng, sem):
        self.eng, self.sem, self.n = eng, sem, 0

    def __call__(self, ins):
        self.n += 1
        ins.then_inc(self.sem, 1)
        self.eng.wait_ge(self.sem, self.n)


class Banks:

    def __init__(self, first, count, filled, emptied_even, emptied_odd):
        self.first, self.count = first, count
        self.filled, self.emptied = filled, (emptied_even, emptied_odd)

    def bank(self, n):
        return self.first + n % self.count

    def claim(self, pe, n):
        if n >= self.count:
            pe.wait_ge(self.emptied[n % 2], (n - self.count) // 2 + 1)

    def take(self, eng, n):
        eng.wait_ge(self.filled, n + 1)

    def all_out(self, eng, n):
        if n:
            eng.wait_ge(self.emptied[0], (n + 1) // 2)
        if n > 1:
            eng.wait_ge(self.emptied[1], n // 2)


class Stream:

    def __init__(self, ring, loaded):
        self.ring, self.loaded = ring, loaded
        self.chunks, self.issued = [], 0
        self.cleared = 0

    def enter(self, src, kc, width, done, value):
        self.chunks.append((src, kc, width, done, value))
        return len(self.chunks) - 1

    def slot(self, n):
        _, kc, width, _, _ = self.chunks[n]
        return self.ring[:, n % WSLOTS, 0:kc * width].rearrange("p (c n) -> p c n", c=kc)

    def load(self, sp, end, ahead=WSLOTS):
        for n in range(self.issued, min(len(self.chunks), end + ahead)):
            if n - WSLOTS >= self.cleared:
                _, _, _, done, value = self.chunks[n - WSLOTS]
                sp.wait_ge(done, value)
            sp.dma_start(self.slot(n), self.chunks[n][0].rearrange("(p c) n -> p c n", c=self.chunks[n][1])).then_inc(self.loaded[n % WSLOTS], 16)
            self.issued = n + 1

    def take(self, pe, n):
        pe.wait_ge(self.loaded[n % WSLOTS], 16 * (n // WSLOTS + 1))
        return self.slot(n)


def bcast_rows(ap, n):
    return ap.rearrange("(a n) -> a n", a=1).broadcast_to((n, ap.shape[0]))


class Modulation:
    CHUNKS = 6 * D // 512
    SLOTS = 4

    def __init__(self, net, first, count, banks):
        self.net, self.first, self.count, self.banks = net, first, count, banks
        self.rows, self.bias = net.modulation_rows
        self.s_mm, self.s_raw, self.s_row = net.modulation_sems
        self.s_bias, self.s_out = net.s_bias, net.s_rows_stored
        self.at = [net.stream.enter(net.a["ada_w"][self.layer(i)][:, self.cols(i)], KC, 512, self.s_mm, first + i + 1) for i in range(count)]
        self.end = self.at[-1] + 1

    def layer(self, i):
        return (self.first + i) // self.CHUNKS

    def cols(self, i):
        at = (self.first + i) % self.CHUNKS * 512
        return slice(at, at + 512)

    def load_bias(self, sp):
        for i in range(self.count):
            n = self.first + i
            if n >= self.SLOTS:
                sp.wait_ge(self.s_row, n - self.SLOTS + 1)
            sp.dma_start(self.bias[:, n % self.SLOTS, :], bcast_rows(self.net.a["ada_b"][self.layer(i)][self.cols(i)], 2)).then_inc(self.s_bias[n % self.SLOTS], 16)

    def product(self, pe, i):
        w = self.net.stream.take(pe, self.at[i])
        if i >= len(self.banks):
            pe.wait_ge(self.s_raw, self.first + i - len(self.banks) + 1)
        for c in range(KC):
            mm = pe.matmul(self.net.ps[0:2, self.banks[i % len(self.banks)], :], self.net.silu_c[:, :, c], w[:, c, :], start=(c == 0), stop=(c == KC - 1))
        mm.then_inc(self.s_mm, 1)

    def copy_out(self, act, i):
        n = self.first + i
        act.wait_ge(self.s_mm, n + 1)
        if n >= self.SLOTS:
            act.wait_ge(self.s_out[n % self.SLOTS], 16 * (n // self.SLOTS))
        act.activation(self.rows[:, n % self.SLOTS, :], self.net.ps[0:2, self.banks[i % len(self.banks)], :], ACT.Copy).then_inc(self.s_raw, 1)

    def add_bias(self, pool):
        for n in range(self.first, self.first + self.count):
            m = n % self.SLOTS
            pool.wait_ge(self.s_bias[m], 16 * (n // self.SLOTS + 1))
            pool.wait_ge(self.s_raw, n + 1)
            pool.tensor_tensor(self.rows[:, m, :], self.rows[:, m, :], self.bias[:, m, :], ALU.add).then_inc(self.s_row, 1)

    def store(self, sp):
        for i in range(self.count):
            n = self.first + i
            sp.wait_ge(self.s_row, n + 1)
            sp.dma_start(self.net.ada_dram[self.layer(i)][:, self.cols(i)], self.rows[:, n % self.SLOTS, :]).then_inc(self.s_out[n % self.SLOTS], 16)


class Net:
    def __init__(self, nc, a, out):
        self.nc, self.a, self.out = nc, a, out
        self.root = ExitStack()
        self.serial = 0
        self.used = []

    def clear_semaphores(self):
        self.nc.clear_and_free_semaphores(self.used)
        self.nc.all_engine_barrier()
        self.used = []
        self.stream.cleared = self.behind

    def sb(self, stack, name, shape, dt=F32):
        self.serial += 1
        return stack.enter_context(self.nc.sbuf_tensor(f"{name}_{self.serial}", shape, dt))

    def sem(self, stack, name):
        self.serial += 1
        sem = self.nc.alloc_semaphore(f"{name}_{self.serial}")
        self.used.append(sem)
        return sem

    def banks(self, st, first, count):
        return Banks(first, count, self.sem(st, "bank_filled"), self.sem(st, "bank_emptied_dve"),
                     self.sem(st, "bank_emptied_act"))

    def k(self, name):
        at, n = CONST[name]
        return self.const[:, at:at + n]

    def build(self):
        nc, root = self.nc, self.root
        with root:
            self.ps = root.enter_context(nc.psum_tensor("ps", [P, 8, 512], F32))
            self.const = self.sb(root, "const", [P, self.a["const"].shape[1]])
            self.h = self.sb(root, "h", [P, NT, D])
            self.ring = self.sb(root, "ring", [P, WSLOTS, WSLOT])
            self.ada_dram = nc.dram_tensor("ada_rows", (2, 2, 6 * D), F32).ap()
            self.v_dram = nc.dram_tensor("v_rows", (NT * P, D), F32).ap()
            self.y_dram = nc.dram_tensor("expert_rows", (NT * P * TOPK, D), F32).ap()
            self.silu_c = self.sb(root, "silu_c", [P, 2, KC])
            self.stream = Stream(self.ring, [nc.alloc_semaphore(f"weights_loaded{i}") for i in range(WSLOTS)])
            self.modulation_sems = [nc.alloc_semaphore(n) for n in ("modulation_product", "product_out", "modulation_row")]
            self.s_bias = [nc.alloc_semaphore(f"bias_loaded{i}") for i in range(Modulation.SLOTS)]
            self.s_rows_stored = [nc.alloc_semaphore(f"rows_stored{i}") for i in range(Modulation.SLOTS)]
            self.modulation_rows = [self.sb(root, n, [2, Modulation.SLOTS, 512]) for n in ("modulation_rows", "modulation_bias")]
            self.behind = 0
            self.layer0()
            self.clear_semaphores()
            self.layer1()
            self.used += self.stream.loaded + self.modulation_sems + self.s_bias + self.s_rows_stored
            self.clear_semaphores()

    def rows_alone(self, block, rows):
        @block.tensor
        def _(pe):
            for i in range(rows.count):
                rows.product(pe, i)

        @block.gpsimd
        def _(pool):
            rows.add_bias(pool)

    def first_rows(self, rows):
        nc, a = self.nc, self.a
        with ExitStack() as st:
            cT = self.sb(st, "cT", [P, 2, KC])
            s_c, s_in, s_silu = (self.sem(st, n) for n in ("c_loaded", "x_loaded", "silu_done"))
            with nc.Block() as block:
                @block.sync
                def _(sp):
                    sp.dma_start(cT[:, 0, :], a["c"][0].rearrange("(p c) -> p c", c=KC)).then_inc(s_c, 16)
                    sp.dma_start(cT[:, 1, :], a["c_ctx"].rearrange("(p c) -> p c", c=KC)).then_inc(s_c, 16)
                    self.behind = rows.end
                    self.stream.load(sp, rows.end, 1)
                    sp.dma_start(self.const[:], a["const"]).then_inc(s_in, 16)
                    for t in range(NT):
                        src = a["x"][0] if t < NL else a["ctx"][0]
                        sp.dma_start(self.h[:, t, :], src[(t % NL) * P:(t % NL + 1) * P, :]).then_inc(s_in, 16)
                    rows.load_bias(sp)
                    rows.store(sp)
                    sp.wait_ge(s_in, 16 * (1 + NT))

                @block.scalar
                def _(act):
                    act.wait_ge(s_c, 32)
                    act.activation(self.silu_c[:], cT[:], ACT.Silu).then_inc(s_silu, 1)
                    for i in range(4):
                        rows.copy_out(act, i)

                @block.tensor
                def _(pe):
                    pe.wait_ge(s_silu, 1)
                    for i in range(4):
                        rows.product(pe, i)

                @block.gpsimd
                def _(pool):
                    rows.add_bias(pool)

    def rows_stored(self, sp, layer, ffn, parts):
        for part in parts:
            for n in range(2):
                n += Modulation.CHUNKS * layer + 2 * (3 * int(ffn) + part)
                sp.wait_ge(self.s_rows_stored[n % Modulation.SLOTS], 16 * (n // Modulation.SLOTS + 1))

    def modulation(self, first, count, banks=(4, 5, 6, 7)):
        return Modulation(self, first, count, banks)

    def inverse_rms(self, chain, act, src, junk, ss, r, size):
        chain(act.activation(junk, src, ACT.Square, accum_out=ss))
        chain(act.activation(ss, ss, ACT.Ln, scale=1.0 / size, bias=self.k("eps")))
        return act.activation(r, ss, ACT.Exp, scale=-0.5)

    def norm_modulate(self, layer, ffn, tiles, u, uT, rows=None):
        nc, a, ps = self.nc, self.a, self.ps
        g_row = a["norm_ffn_pre" if ffn else "norm_mix_pre"][layer]
        groups = sorted({t // NL for t in tiles})
        with ExitStack() as st:
            g = self.sb(st, "gain", [P, D])
            scale = self.sb(st, "scale", [P, 2, D])
            shift = self.sb(st, "shift", [P, 2, D])
            junk = self.sb(st, "squares", [P, D])
            ss = self.sb(st, "ss", [P, NT])
            r = self.sb(st, "r", [P, NT])
            s_g, s_r, s_u, s_c, s_a = (self.sem(st, n) for n in ("rows_loaded", "r_ready", "u_ready", "dve_chain", "act_chain"))
            bk = self.banks(st, 0, 4)

            def row(group, part):
                at = (3 * int(ffn) + part) * D
                return bcast_rows(self.ada_dram[layer, group, at:at + D], P)

            with nc.Block() as block:
                @block.sync
                def _(sp):
                    sp.dma_start(g[:], bcast_rows(g_row, P)).then_inc(s_g, 16)
                    self.rows_stored(sp, layer, ffn, (0, 1))
                    for i in groups:
                        sp.dma_start(scale[:, i, :], row(i, 1)).then_inc(s_g, 16)
                        sp.dma_start(shift[:, i, :], row(i, 0)).then_inc(s_g, 16)
                    self.beside_sp(sp, rows, 1 if ffn else WSLOTS)
                    sp.wait_ge(s_g, 16 * (1 + 2 * len(groups)))

                if rows:
                    @block.gpsimd
                    def _(pool):
                        rows.add_bias(pool)

                @block.scalar
                def _(act):
                    act.preload_act_table_set("natural_log_exp_and_others")
                    chain = Chain(act, s_a)
                    for t in tiles:
                        self.inverse_rms(chain, act, self.h[:, t, :], junk[:], ss[:, t:t + 1], r[:, t:t + 1], D).then_inc(s_r, 1)
                    if rows:
                        rows.copy_out(act, 0)
                    for n in range(1, 2 * len(tiles), 2):
                        if rows and n // 2 + 1 < rows.count:
                            rows.copy_out(act, n // 2 + 1)
                        bk.take(act, n)
                        dst = uT[:, 4:8, tiles[n // 2] * P:(tiles[n // 2] + 1) * P]
                        act.activation(dst, ps[:, bk.bank(n), :].rearrange("p (c t) -> p c t", c=4), ACT.Copy).then_inc(bk.emptied[1], 1)

                @block.vector
                def _(dve):
                    chain = Chain(dve, s_c)

                    def copy_out(dve, n):
                        bk.take(dve, n)
                        dst = uT[:, 0:4, tiles[n // 2] * P:(tiles[n // 2] + 1) * P]
                        dve.tensor_copy(dst, ps[:, bk.bank(n), :].rearrange("p (c t) -> p c t", c=4)).then_inc(bk.emptied[0], 1)

                    dve.wait_ge(s_g, 16 * (1 + 2 * len(groups)))
                    for i in groups:
                        chain(dve.scalar_tensor_tensor(scale[:, i, :], scale[:, i, :], 1.0, g[:], ALU.add, ALU.mult))
                    for i, t in enumerate(tiles):
                        dve.wait_ge(s_r, i + 1)
                        chain(dve.scalar_tensor_tensor(u[:, t, :], self.h[:, t, :], r[:, t:t + 1], scale[:, t // NL, :], ALU.mult, ALU.mult))
                        dve.tensor_tensor(u[:, t, :], u[:, t, :], shift[:, t // NL, :], ALU.add).then_inc(s_u, 1)
                        if i >= 2:
                            copy_out(dve, 2 * (i - 2))
                    for i in range(len(tiles) - 2, len(tiles)):
                        copy_out(dve, 2 * i)

                @block.tensor
                def _(pe):
                    if rows:
                        rows.product(pe, 0)
                    for i, t in enumerate(tiles):
                        if rows and i + 1 < rows.count:
                            rows.product(pe, i + 1)
                        pe.wait_ge(s_u, i + 1)
                        x = u[:, t, :].rearrange("p (q c) -> p c q", c=KC)
                        for half in range(2):
                            n = 2 * i + half
                            bk.claim(pe, n)
                            for c in range(4):
                                mm = pe.transpose(ps[:, bk.bank(n), c * P:(c + 1) * P], x[:, 4 * half + c, :], self.k("ident"))
                            mm.then_inc(bk.filled, 1)

    def beside_sp(self, sp, rows, ahead=WSLOTS):
        if rows:
            rows.load_bias(sp)
            self.behind = rows.end
        self.stream.load(sp, self.behind, ahead)
        if rows:
            rows.store(sp)

    def residual(self, layer, ffn, tiles, o, rows=None):
        nc, a = self.nc, self.a
        g_row = a["norm_ffn_post" if ffn else "norm_mix_post"][layer]
        groups = sorted({t // NL for t in tiles})
        with ExitStack() as st:
            g = self.sb(st, "gain", [P, D])
            gate = self.sb(st, "gate", [P, 2, D])
            junk = self.sb(st, "squares", [P, D])
            ss = self.sb(st, "ss", [P, NT])
            r = self.sb(st, "r", [P, NT])
            s_g, s_r, s_c, s_a = (self.sem(st, n) for n in ("rows_loaded", "r_ready", "dve_chain", "act_chain"))
            with nc.Block() as block:
                if rows:
                    self.rows_alone(block, rows)

                @block.sync
                def _(sp):
                    sp.dma_start(g[:], bcast_rows(g_row, P)).then_inc(s_g, 16)
                    self.rows_stored(sp, layer, ffn, (2,))
                    for i in groups:
                        at = (3 * int(ffn) + 2) * D
                        sp.dma_start(gate[:, i, :], bcast_rows(self.ada_dram[layer, i, at:at + D], P)).then_inc(s_g, 16)
                    self.beside_sp(sp, rows, 1)
                    sp.wait_ge(s_g, 16 * (1 + len(groups)))

                @block.scalar
                def _(act):
                    act.preload_act_table_set("natural_log_exp_and_others")
                    chain = Chain(act, s_a)
                    for t in tiles:
                        self.inverse_rms(chain, act, o[:, t, :], junk[:], ss[:, t:t + 1], r[:, t:t + 1], D).then_inc(s_r, 1)
                    for i in range(rows.count if rows else 0):
                        rows.copy_out(act, i)

                @block.vector
                def _(dve):
                    chain = Chain(dve, s_c)
                    dve.wait_ge(s_g, 16 * (1 + len(groups)))
                    for i in groups:
                        chain(dve.tensor_tensor(gate[:, i, :], gate[:, i, :], g[:], ALU.mult))
                    for i, t in enumerate(tiles):
                        dve.wait_ge(s_r, i + 1)
                        chain(dve.scalar_tensor_tensor(o[:, t, :], o[:, t, :], r[:, t:t + 1], gate[:, t // NL, :], ALU.mult, ALU.mult))
                        chain(dve.tensor_tensor(self.h[:, t, :], self.h[:, t, :], o[:, t, :], ALU.add))

    def plan(self, w, kc, jobs):
        bk = self.banks(None, 0, 8)
        upto = [sum(len(job[2]) for job in jobs[:j + 1]) for j in range(len(jobs))]
        at = [self.stream.enter(w[:, first:first + width], kc, width, bk.filled, upto[j]) for j, (first, width, _) in enumerate(jobs)]
        return bk, at, kc, jobs

    def linear(self, planned, xT):
        nc, ps = self.nc, self.ps
        bk, at, kc, jobs = planned
        items = [(j, i) for j, job in enumerate(jobs) for i in range(len(job[2]))]

        def copies(eng, parity, copy):
            for n, (j, i) in enumerate(items):
                if n % 2 == parity:
                    dst = jobs[j][2][i][1]
                    bk.take(eng, n)
                    copy(dst, ps[0:dst.shape[0], bk.bank(n), 0:dst.shape[1]]).then_inc(bk.emptied[parity], 1)

        with nc.Block() as block:
            @block.sync
            def _(sp):
                self.behind = at[-1] + 1
                self.stream.load(sp, self.behind)

            @block.tensor
            def _(pe):
                for n, (j, i) in enumerate(items):
                    if i == 0:
                        w = self.stream.take(pe, at[j])
                    bk.claim(pe, n)
                    t = jobs[j][2][i][0]
                    for c in range(kc):
                        if t is None:
                            lhs, rhs = w[:, c, i * P:(i + 1) * P], xT[:, c, :]
                        else:
                            lhs, rhs = xT[:, c, t * P:(t + 1) * P], w[:, c, :]
                        mm = pe.matmul(ps[:, bk.bank(n), 0:rhs.shape[1]], lhs, rhs, start=(c == 0), stop=(c == kc - 1))
                    mm.then_inc(bk.filled, 1)

            @block.vector
            def _(dve):
                copies(dve, 0, dve.tensor_copy)

            @block.scalar
            def _(act):
                copies(act, 1, lambda o, i: act.activation(o, i, ACT.Copy))

    def prefetch(self, block):
        @block.sync
        def _(sp):
            self.stream.load(sp, self.behind)

    def transposed(self, jobs):
        nc, ps = self.nc, self.ps
        with ExitStack() as st:
            bk = self.banks(st, 0, 8)

            def copies(eng, parity, copy):
                for n, (dst, srcs, factor) in enumerate(jobs):
                    if n % 2 == parity:
                        bk.take(eng, n)
                        src = ps[0:dst.shape[0], bk.bank(n), 0:len(srcs) * P]
                        if len(dst.shape) == 3:
                            src = src.rearrange("p (c t) -> p c t", t=P)
                        copy(dst, src, factor).then_inc(bk.emptied[parity], 1)

            with nc.Block() as block:
                self.prefetch(block)

                @block.tensor
                def _(pe):
                    for n, (dst, srcs, _) in enumerate(jobs):
                        bk.claim(pe, n)
                        for c, src in enumerate(srcs):
                            mm = pe.transpose(ps[0:dst.shape[0], bk.bank(n), c * P:(c + 1) * P], src, self.k("ident"))
                        mm.then_inc(bk.filled, 1)

                @block.vector
                def _(dve):
                    copies(dve, 0, lambda o, i, f: dve.tensor_scalar(o, i, f, None, ALU.mult) if f != 1.0 else dve.tensor_copy(o, i))

                @block.scalar
                def _(act):
                    copies(act, 1, lambda o, i, f: act.activation(o, i, ACT.Copy, scale=f))

    def transpose_rows(self, src, kc, tiles, dst):
        step = min(4, kc)
        self.transposed([(dst[:, c:c + step, t * P:(t + 1) * P],
                          [src(t).rearrange("p (q c) -> p c q", c=kc)[:, c + i, :] for i in range(step)], 1.0)
                         for t in tiles for c in range(0, kc, step)])

    def attention(self, items, o_of):
        nc, ps = self.nc, self.ps
        maps = [(i, m) for i, it in enumerate(items) for m in range(len(it["q"]))]
        M = len(items[0]["q"])
        with ExitStack() as st:
            prob = self.sb(st, "prob", [P, 4, 512])
            pT = self.sb(st, "prob_T", [P, 2, 4, P])
            top = self.sb(st, "row_max", [P, 4])
            tot = self.sb(st, "row_sum", [P, 4])
            inv = self.sb(st, "row_inv", [P, 4])
            s_s, s_max, s_exp, s_w = (self.sem(st, n) for n in ("scores", "row_max", "exp_done", "weights_ready"))
            s_tr, s_pT, s_pv, s_o, s_c = (self.sem(st, n) for n in ("prob_transposed", "prob_T_ready", "pv_done", "o_ready", "dve_chain"))
            SB, TB, OB = 0, 4, 6

            with nc.Block() as block:
                self.prefetch(block)

                @block.tensor
                def _(pe):
                    def scores(m):
                        i, part = maps[m]
                        it = items[i]
                        if m >= 4:
                            pe.wait_ge(s_exp, m - 3)
                        q, k = it["q"][part], it["k"][part]
                        pe.matmul(ps[:, SB + m % 4, 0:k.shape[1]], q, k, start=True, stop=True).then_inc(s_s, 1)

                    def turn(i):
                        it = items[i]
                        pe.wait_ge(s_exp if M == 1 else s_w, i + 1)
                        if i >= 2:
                            pe.wait_ge(s_pT, i - 1)
                        src = prob[:, (M * i) % 4, :]
                        for c in range(len(it["v"])):
                            tr = pe.transpose(ps[:, TB + i % 2, c * P:(c + 1) * P], src[:, c * P:(c + 1) * P], self.k("ident"))
                        tr.then_inc(s_tr, 1)

                    def values(i):
                        it = items[i]
                        pe.wait_ge(s_pT, i + 1)
                        if i >= 2:
                            pe.wait_ge(s_o, i - 1)
                        n = len(it["v"])
                        for c, v in enumerate(it["v"]):
                            mm = pe.matmul(ps[:, OB + i % 2, 0:v.shape[1]], pT[:, i % 2, c, :], v, start=(c == 0), stop=(c == n - 1))
                        mm.then_inc(s_pv, 1)

                    for i in range(len(items) + 2):
                        if i < len(items):
                            for part in range(M):
                                scores(M * i + part)
                        if 1 <= i <= len(items):
                            turn(i - 1)
                        if i >= 2:
                            values(i - 2)

                @block.vector
                def _(dve):
                    chain = Chain(dve, s_c)

                    def row_max(m):
                        n = items[maps[m][0]]["k"][0].shape[1]
                        dve.wait_ge(s_s, m + 1)
                        if m >= 4:
                            dve.wait_ge(s_exp, m - 3)
                        dve.tensor_reduce(top[:, m % 4:m % 4 + 1], ps[:, SB + m % 4, 0:n], AX, ALU.max, negate=True).then_inc(s_max, 1)

                    def weights(i):
                        n = items[i]["k"][0].shape[1]
                        dve.wait_ge(s_exp, M * (i + 1))
                        a = (M * i) % 4
                        chain(dve.reciprocal(inv[:, a:a + M], tot[:, a:a + M]))
                        if M == 2:
                            chain(dve.tensor_tensor(inv[:, a + 1:a + 2], inv[:, a + 1:a + 2], self.neg_lambda[:], ALU.mult))
                            chain(dve.tensor_scalar(prob[:, a, 0:n], prob[:, a, 0:n], inv[:, a:a + 1], None, ALU.mult))
                            dve.scalar_tensor_tensor(prob[:, a, 0:n], prob[:, a + 1, 0:n], inv[:, a + 1:a + 2], prob[:, a, 0:n],
                                                     ALU.mult, ALU.add).then_inc(s_w, 1)

                    def out(i):
                        a = (M * i) % 4
                        dve.wait_ge(s_pv, i + 1)
                        o = o_of(i)
                        src = ps[:, OB + i % 2, 0:o.shape[1]]
                        if M == 1:
                            dve.tensor_scalar(o, src, inv[:, a:a + 1], None, ALU.mult).then_inc(s_o, 1)
                        else:
                            dve.tensor_copy(o, src).then_inc(s_o, 1)

                    for i in range(len(items) + 2):
                        if i < len(items):
                            for part in range(M):
                                row_max(M * i + part)
                        if 1 <= i <= len(items):
                            weights(i - 1)
                        if i >= 2:
                            out(i - 2)

                @block.scalar
                def _(act):
                    def exp(m):
                        i = maps[m][0]
                        n = items[i]["k"][0].shape[1]
                        act.wait_ge(s_max, m + 1)
                        if m >= 4:
                            act.wait_ge(s_tr, (m - 4) // M + 1)
                            act.wait_ge(s_o, (m - 4) // M + 1)
                        ins = act.activation(prob[:, m % 4, 0:n], ps[:, SB + m % 4, 0:n], ACT.Exp, bias=top[:, m % 4:m % 4 + 1],
                                             accum_out=tot[:, m % 4:m % 4 + 1])
                        ins.then_inc(s_exp, 1)

                    def copy(i):
                        n = len(items[i]["v"])
                        act.wait_ge(s_tr, i + 1)
                        if i >= 2:
                            act.wait_ge(s_pv, i - 1)
                        act.activation(pT[:, i % 2, 0:n, :], ps[:, TB + i % 2, 0:n * P].rearrange("p (c t) -> p c t", t=P),
                                       ACT.Copy).then_inc(s_pT, 1)

                    for i in range(len(items) + 1):
                        if i < len(items):
                            for part in range(M):
                                exp(M * i + part)
                        if i >= 1:
                            copy(i - 1)

    def rope(self, chain, dve, x, tmp, dim, t):
        heads = x.shape[1]
        cos = self.k(f"cos{dim}")[:, t * dim:(t + 1) * dim]
        sin = self.k(f"sin{dim}")[:, t * dim:(t + 1) * dim]
        u = dim // 4
        tmp = tmp[:, 0:heads * dim].rearrange("p (h d) -> p h d", d=dim)
        for half in range(2):
            for s in range(2):
                o = half * 2 * u + s * u
                i = half * 2 * u + (1 - s) * u
                sn = sin[:, o:o + u].rearrange("p (a u) -> p a u", a=1).broadcast_to((P, heads, u))
                ins = dve.tensor_tensor(tmp[:, :, o:o + u], x[:, :, i:i + u], sn, ALU.mult)
                chain(ins)
        cs = cos.rearrange("p (a u) -> p a u", a=1).broadcast_to((P, heads, dim))
        chain(dve.tensor_tensor(x, x, cs, ALU.mult))
        return dve.tensor_tensor(x, x, tmp, ALU.add)

    def layer0(self):
        a, tiles = self.a, list(range(NT))
        with ExitStack() as st:
            o = self.sb(st, "o", [P, NT, D])
            first, rows = self.modulation(0, 4), self.modulation(4, 2)
            self.first_rows(first)
            with ExitStack() as s1:
                proj = self.sb(s1, "proj", [P, NT, ATT_IN])
                with ExitStack() as s2:
                    uT = self.sb(s2, "uT", [P, KC, NT * P])
                    jobs = [(n, min(512, ATT_IN - n), [(t, proj[:, t, n:min(n + 512, ATT_IN)]) for t in tiles])
                            for n in range(0, ATT_IN, 512)]
                    planned = self.plan(a["att_w_in"][0], KC, jobs)
                    self.norm_modulate(0, False, tiles, o, uT, rows)
                    self.latent_rows = self.modulation(6, 3)
                    self.linear(planned, uT)
                q = self.sb(s1, "q", [P, NT, MH * QK])
                kv = self.sb(s1, "kv", [P, NT, MH * (NOPE + MV)])
                self.latents(proj, q, kv, tiles)
                kz = self.sb(s1, "gqa_keys_padded", [P, NT, GKV, 3 * GD])
                self.mla_heads(proj, q, kv, kz, o)
                jobs = [(n, 512, [(t, o[:, t, n:n + 512]) for t in tiles]) for n in (0, 512)]
                w_out = self.plan(a["mix_w_out"][0], KC, jobs)
                self.gqa_heads(proj, kz, o)
            if self.stop("att"):
                return
            with ExitStack() as s1:
                oT = self.sb(s1, "oT", [P, KC, NT * P])
                self.transpose_rows(lambda t: o[:, t, :], KC, tiles, oT)
                mix_rows, ffn_rows = self.modulation(12, 2), self.modulation(14, 2)
                self.linear(w_out, oT)
            self.residual(0, False, tiles, o, mix_rows)
        if self.stop("mix0"):
            return
        self.clear_semaphores()
        self.experts(0, tiles, P, ffn_rows)

    def latents(self, proj, q, kv, tiles):
        nc, a = self.nc, self.a
        H10 = GH + GKV
        with ExitStack() as st:
            rows = self.latent_rows
            jobs = [(n, w, [(t, q[:, t, n:n + w]) for t in tiles]) for n, w in ((0, 512), (512, 256))]
            q_up = self.plan(a["mla_w_q_up"][0], 2, jobs)
            jobs = [(n, 512, [(t, kv[:, t, n:n + 512]) for t in tiles]) for n in (0, 512)]
            kv_up = self.plan(a["mla_w_kv_up"][0], 1, jobs)
            lat = self.sb(st, "latents", [P, NT, QLORA + KVLORA])
            latT = self.sb(st, "latents_T", [P, 3, NT * P])
            gq = self.sb(st, "q_gain", [P, QLORA])
            gkv = self.sb(st, "kv_gain", [P, KVLORA])
            gh = self.sb(st, "head_gain", [P, 2, GD])
            ss = self.sb(st, "ss", [P, NT, 2 + H10])
            r = self.sb(st, "r", [P, NT, 2 + H10])
            junk = self.sb(st, "squares", [P, H10 * GD])
            s_g, s_r, s_c, s_a, s_sq, s_ss = (self.sem(st, n) for n in ("gains_loaded", "r_ready", "dve_chain", "act_chain", "squares", "sums"))
            with nc.Block() as block:
                self.rows_alone(block, rows)

                @block.sync
                def _(sp):
                    sp.dma_start(gq[:], bcast_rows(a["mla_q_norm"][0], P)).then_inc(s_g, 16)
                    sp.dma_start(gkv[:], bcast_rows(a["mla_kv_norm"][0], P)).then_inc(s_g, 16)
                    sp.dma_start(gh[:, 0, :], bcast_rows(a["gqa_q_norm"][0], P)).then_inc(s_g, 16)
                    sp.dma_start(gh[:, 1, :], bcast_rows(a["gqa_k_norm"][0], P)).then_inc(s_g, 16)
                    self.beside_sp(sp, rows)
                    sp.wait_ge(s_g, 64)

                @block.scalar
                def _(act):
                    act.preload_act_table_set("natural_log_exp_and_others")
                    chain = Chain(act, s_a)
                    for i, t in enumerate(tiles):
                        if i:
                            act.wait_ge(s_ss, i)
                        chain(act.activation(junk[:, 0:QLORA], proj[:, t, 0:QLORA], ACT.Square, accum_out=ss[:, t, 0:1]))
                        chain(act.activation(junk[:, 0:KVLORA], proj[:, t, C_KV:C_PE], ACT.Square, accum_out=ss[:, t, 1:2]))
                        act.activation(junk[:], proj[:, t, C_GQ:C_GV], ACT.Square).then_inc(s_sq, 1)
                        act.wait_ge(s_ss, i + 1)
                        act.activation(ss[:, t, 0:1], ss[:, t, 0:1], ACT.Ln, scale=1.0 / QLORA, bias=self.k("eps"))
                        act.activation(ss[:, t, 1:2], ss[:, t, 1:2], ACT.Ln, scale=1.0 / KVLORA, bias=self.k("eps"))
                        chain(act.activation(ss[:, t, 2:], ss[:, t, 2:], ACT.Ln, scale=1.0 / GD, bias=self.k("eps")))
                        act.activation(r[:, t, :], ss[:, t, :], ACT.Exp, scale=-0.5).then_inc(s_r, 1)
                    for i in range(rows.count):
                        rows.copy_out(act, i)

                @block.vector
                def _(dve):
                    chain = Chain(dve, s_c)
                    dve.wait_ge(s_g, 64)
                    for i, t in enumerate(tiles):
                        dve.wait_ge(s_sq, i + 1)
                        dve.tensor_reduce(ss[:, t, 2:], junk[:].rearrange("p (h d) -> p h d", d=GD), AX, ALU.add).then_inc(s_ss, 1)
                        dve.wait_ge(s_r, i + 1)
                        chain(dve.scalar_tensor_tensor(lat[:, t, 0:QLORA], proj[:, t, 0:QLORA], r[:, t, 0:1], gq[:], ALU.mult, ALU.mult))
                        chain(dve.scalar_tensor_tensor(lat[:, t, QLORA:], proj[:, t, C_KV:C_PE], r[:, t, 1:2], gkv[:], ALU.mult, ALU.mult))
                        heads = proj[:, t, C_GQ:C_GV].rearrange("p (h d) -> p h d", d=GD)
                        rb = r[:, t, 2:].rearrange("p (h a) -> p h a", a=1).broadcast_to((P, H10, GD))
                        chain(dve.tensor_tensor(heads, heads, rb, ALU.mult))
                        for lo, hi, g in ((0, GH, 0), (GH, H10, 1)):
                            gb = gh[:, g:g + 1, :].broadcast_to((P, hi - lo, GD))
                            chain(dve.tensor_tensor(heads[:, lo:hi, :], heads[:, lo:hi, :], gb, ALU.mult))
            self.transpose_rows(lambda t: lat[:, t, 0:QLORA], 2, tiles, latT[:, 0:2, :])
            self.transpose_rows(lambda t: lat[:, t, QLORA:], 1, tiles, latT[:, 2:3, :])
            self.mla_rows = self.modulation(9, 3)
            self.linear(q_up, latT[:, 0:2, :])
            self.linear(kv_up, latT[:, 2:3, :])

    def mla_heads(self, proj, q, kv, kz, o):
        nc = self.nc
        with ExitStack() as st:
            qT = self.sb(st, "qT", [QK, MH, NT * P])
            kT = self.sb(st, "kT", [QK, MH, NT * P])
            with ExitStack() as s1:
                tmp = self.sb(s1, "swapped", [P, (GH + GKV) * GD])
                kf = self.sb(s1, "k_heads", [P, NT, MH, QK])
                rows = self.mla_rows
                s_c, s_pe = self.sem(st, "dve_chain"), self.sem(st, "k_pe_ready")
                s_kf, s_kz = self.sem(st, "keys_assembled"), self.sem(st, "zeros_written")
                with nc.Block() as block:
                    self.rows_alone(block, rows)

                    @block.sync
                    def _(sp):
                        self.beside_sp(sp, rows)

                    @block.vector
                    def _(dve):
                        chain = Chain(dve, s_c)
                        dve.memset(kz[:], 0.0).then_inc(s_kz, 1)
                        for t in range(NL):
                            self.rope(chain, dve, proj[:, t, C_PE:C_GQ].rearrange("p (h d) -> p h d", h=1), tmp, ROPE, t).then_inc(s_pe, 1)
                            dve.wait_ge(s_pe, t + 1)
                        for t in range(NL):
                            qpe = q[:, t, :].rearrange("p (h d) -> p h d", h=MH)[:, :, NOPE:]
                            chain(self.rope(chain, dve, qpe, tmp, ROPE, t))
                            chain(self.rope(chain, dve, proj[:, t, C_GQ:C_GV].rearrange("p (h d) -> p h d", d=GD), tmp, GD, t))
                        dve.wait_ge(s_kz, 1)
                        chain(dve.tensor_copy(kz[:, :, :, GD:2 * GD], proj[:, :, C_GK:C_GV].rearrange("p t (g d) -> p t g d", g=GKV)))

                    @block.scalar
                    def _(act):
                        for t in range(NT):
                            kvt = kv[:, t, :].rearrange("p (h d) -> p h d", h=MH)
                            act.activation(kf[:, t, :, 0:NOPE], kvt[:, :, 0:NOPE], ACT.Copy).then_inc(s_kf, 1)
                            if t < NL:
                                act.wait_ge(s_pe, t + 1)
                            pe_ = proj[:, t, C_PE:C_GQ].rearrange("p (h d) -> p h d", h=1).broadcast_to((P, MH, ROPE))
                            act.activation(kf[:, t, :, NOPE:], pe_, ACT.Copy).then_inc(s_kf, 1)
                        act.wait_ge(s_kf, 2 * NT)
                        for i in range(rows.count):
                            rows.copy_out(act, i)
                jobs = []
                for h in range(MH):
                    jobs.append((qT[:, h, :], [q[:, t, h * QK:(h + 1) * QK] for t in range(NT)], QK ** -0.5))
                    jobs.append((kT[:, h, :], [kf[:, t, h, :] for t in range(NT)], 1.0))
                self.transposed(jobs)
            items, outs = [], []
            for h in range(MH):
                for t in range(NT):
                    keys = range(NT) if t < NL else range(NL, NT)
                    v = [kv[:, s, h * (NOPE + MV) + NOPE:(h + 1) * (NOPE + MV)] for s in keys]
                    items.append({"q": [qT[:, h, t * P:(t + 1) * P]], "k": [kT[:, h, keys[0] * P:NT * P]], "v": v})
                    outs.append(o[:, t, h * MV:(h + 1) * MV])
            self.attention(items, lambda i: outs[i])

    def gqa_heads(self, proj, kz, o):
        with ExitStack() as st:
            qT = self.sb(st, "qT", [2 * GD, GH // 2, NT * P])
            kT = self.sb(st, "kT", [2 * GD, GKV, 2, NT * P])
            jobs = [(qT[:, h // 2, :], [proj[:, t, C_GQ + h * GD:C_GQ + (h + 2) * GD] for t in range(NT)], GD ** -0.5)
                    for h in range(0, GH, 2)]
            jobs += [(kT[:, g, odd, :], [kz[:, t, g, (1 - odd) * GD:(3 - odd) * GD] for t in range(NT)], 1.0)
                     for g in range(GKV) for odd in range(2)]
            self.transposed(jobs)
            items, outs = [], []
            for h in range(GH):
                g = h // (GH // GKV)
                for t in range(NT):
                    keys = range(NT) if t < NL else range(NL, NT)
                    v = [proj[:, s, C_GV + g * GD:C_GV + (g + 1) * GD] for s in keys]
                    items.append({"q": [qT[:, h // 2, t * P:(t + 1) * P]], "k": [kT[:, g, h % 2, keys[0] * P:NT * P]], "v": v})
                    outs.append(o[:, t, MH * MV + h * GD:MH * MV + (h + 1) * GD])
            self.attention(items, lambda i: outs[i])

    def stop(self, stage):
        return False

    def experts(self, layer, tiles, slots, rows=None):
        n = len(tiles)
        with ExitStack() as st:
            vT = self.sb(st, "vT", [P, KC, n * P])
            self.key = self.sb(st, "slot_of_expert", [P, NT, NE])
            self.w8 = self.sb(st, "weight8", [P, NT, TOPK])
            self.weight = self.sb(st, "weight_of_expert", [P, NT, NE])
            self.place = self.sb(st, "place_of_expert", [P, NT, NE])
            self.block_expert = self.sb(st, "block_expert", [1, BLOCKS + 8], I32)
            self.turns = self.sb(st, "turns", [1, 1], I32)
            self.block_first = self.sb(st, "block_first", [P, BLOCKS + 8])
            more_rows = self.modulation(16, 2, banks=(3,)) if layer == 0 else None
            with ExitStack() as s1:
                v = self.sb(s1, "v", [P, n, D])
                self.norm_modulate(layer, True, tiles, v, vT, rows)
                self.route(layer, n, slots, v, vT, more_rows)
            self.expert_blocks(layer, n, slots)
            rows = self.modulation(18, 1) if layer == 0 else None
            f = self.sb(st, "f", [P, n, D])
            self.combine(layer, n, f, vT)
            self.residual(layer, True, tiles, f, rows)

    def route(self, layer, n, slots, v, vT, rows=None):
        nc, a, ps = self.nc, self.a, self.ps
        with ExitStack() as st:
            rw = self.sb(st, "router_w", [P, KC, NE])
            rb = self.sb(st, "router_b", [P, NE])
            score = self.sb(st, "score", [P, n, NE])
            sel = self.sb(st, "selection_score", [P, NE])
            masked = self.sb(st, "masked", [P, NE])
            left = self.sb(st, "left", [P, NE])
            top8 = self.sb(st, "top8", [P, NG, 8])
            grp = self.sb(st, "group_score", [P, NG])
            cmp1 = self.sb(st, "compare", [P, NG, NG])
            cmp2 = self.sb(st, "compare_equal", [P, NG, NG])
            chosen = self.sb(st, "chosen", [P, n, NE])
            wsum = self.sb(st, "weight_sum", [P, n])
            k8 = self.sb(st, "key8", [P, 8])
            hit = self.sb(st, "hit", [P, 8, NE])
            col = self.sb(st, "blocks_of_expert", [NE, 1])
            count = self.sb(st, "count", [NE, 2])
            wide = self.sb(st, "counts_wide", [NE, 2, P])
            more = self.sb(st, "more_than", [NE, NT])
            begun = self.sb(st, "ended_before", [NE, BLOCKS + 8])
            first = self.sb(st, "first_slot", [P, NE])
            one = self.sb(st, "one_row", [1, BLOCKS + 8])
            total = self.sb(st, "total", [1, 2])
            (s_in, s_lg, s_e, s_c, s_ch, s_rank, s_col, s_wide, s_cum, s_beg, s_bx, s_v) = (self.sem(st, x) for x in (
                "router_loaded", "logits", "exp_done", "dve_chain", "chosen_ready", "ranks", "blocks_ready", "blocks_wide",
                "blocks_summed", "ended_ready", "block_experts", "v_stored"))
            LB, RB, CB, XB = 4, 0, 1, 2
            with nc.Block() as block:
                @block.sync
                def _(sp):
                    sp.dma_start(rw[:], a["router_w"][layer].rearrange("(p c) e -> p c e", c=KC)).then_inc(s_in, 16)
                    sp.dma_start(rb[:], bcast_rows(a["router_b"][layer], P)).then_inc(s_in, 16)
                    for t in range(n):
                        sp.dma_start(self.v_dram[t * P:(t + 1) * P, :], v[:, t, :]).then_inc(s_v, 16)
                    self.beside_sp(sp, rows)
                    sp.wait_ge(s_in, 32)
                    sp.wait_ge(s_v, 16 * n)

                if rows:
                    @block.gpsimd
                    def _(pool):
                        rows.add_bias(pool)

                @block.tensor
                def _(pe):
                    pe.wait_ge(s_in, 32)
                    for t in range(n):
                        for c in range(KC):
                            mm = pe.matmul(ps[:, LB + t, 0:NE], vT[:, c, t * P:(t + 1) * P], rw[:, c, :],
                                           start=(c == 0), stop=(c == KC - 1))
                        mm.then_inc(s_lg, 1)
                    for t in range(n):
                        if rows and t < rows.count:
                            rows.product(pe, t)
                        pe.wait_ge(s_ch, t + 1)
                        for s in range(t + 1):
                            mm = pe.matmul(ps[:, RB, t * NE:(t + 1) * NE], self.k("tri_lt" if s == t else "ones"), chosen[:, s, :],
                                           start=(s == 0), stop=(s == t))
                    for s in range(n):
                        mm = pe.matmul(ps[0:NE, CB, 0:1], chosen[:, s, :], self.k("one"), start=(s == 0), stop=(s == n - 1))
                    mm.then_inc(s_rank, 1)
                    pe.wait_ge(s_wide, 1)
                    pe.matmul(ps[:, CB, 64:64 + NE], wide[:, 0, :], self.k("tri_lt")[0:NE, 0:NE], start=True, stop=True)
                    pe.matmul(ps[0:NE, CB, 1:2], self.k("tri_le")[0:NE, 0:NE], col[:], start=True, stop=True)
                    pe.matmul(ps[0:1, CB, 2:3], col[:], self.k("one")[0:NE, :], start=True, stop=True).then_inc(s_cum, 1)
                    pe.wait_ge(s_beg, 1)
                    pe.matmul(ps[0:1, XB, 0:BLOCKS + 8], self.k("one")[0:NE, :], begun[:], start=True, stop=True)
                    pe.matmul(ps[:, XB, 128:128 + BLOCKS + 8], wide[:, 1, :], begun[:], start=True, stop=True).then_inc(s_bx, 1)

                @block.scalar
                def _(act):
                    for t in range(n):
                        act.wait_ge(s_lg, t + 1)
                        act.activation(score[:, t, :], ps[:, LB + t, 0:NE], ACT.Exp, scale=-1.0).then_inc(s_e, 1)
                    for i in range(rows.count if rows else 0):
                        rows.copy_out(act, i)

                @block.vector
                def _(dve):
                    chain = Chain(dve, s_c)
                    dve.wait_ge(s_in, 32)
                    for t in range(n):
                        dve.wait_ge(s_e, t + 1)
                        sc = score[:, t, :]
                        chain(dve.tensor_scalar(sc, sc, 1.0, None, ALU.add))
                        chain(dve.reciprocal(sc, sc))
                        chain(dve.tensor_tensor(sel[:], sc, rb[:], ALU.add))
                        for g in range(NG):
                            ins = dve.max(top8[:, g, :], sel[:, g * 8:(g + 1) * 8])
                        chain(ins)
                        chain(dve.tensor_tensor(grp[:], top8[:, :, 0], top8[:, :, 1], ALU.add))
                        mine = grp[:].rearrange("p (g a) -> p g a", a=1).broadcast_to((P, NG, NG))
                        other = grp[:].rearrange("p (a g) -> p a g", a=1).broadcast_to((P, NG, NG))
                        chain(dve.tensor_tensor(cmp1[:], other, mine, ALU.is_gt))
                        chain(dve.tensor_tensor(cmp2[:], other, mine, ALU.is_equal))
                        chain(dve.tensor_tensor(cmp2[:], cmp2[:], self.k("lower").rearrange("p (g q) -> p g q", g=NG), ALU.mult))
                        chain(dve.tensor_tensor(cmp1[:], cmp1[:], cmp2[:], ALU.add))
                        chain(dve.tensor_reduce(grp[:], cmp1[:], AX, ALU.add))
                        chain(dve.tensor_scalar(grp[:], grp[:], float(TG), None, ALU.is_lt))
                        stay = grp[:].rearrange("p (g a) -> p g a", a=1).broadcast_to((P, NG, NE // NG))
                        chain(dve.tensor_tensor(masked[:].rearrange("p (g e) -> p g e", g=NG), sel[:].rearrange("p (g e) -> p g e", g=NG), stay, ALU.mult))
                        chain(dve.tensor_scalar(grp[:], grp[:], -NEG, NEG, ALU.mult, ALU.add))
                        chain(dve.tensor_tensor(masked[:].rearrange("p (g e) -> p g e", g=NG), masked[:].rearrange("p (g e) -> p g e", g=NG), stay, ALU.add))
                        chain(dve.max(k8[:], masked[:]))
                        chain(dve.match_replace(left[:], k8[:], masked[:], GONE))
                        dve.tensor_tensor(chosen[:, t, :], left[:], masked[:], ALU.not_equal).then_inc(s_ch, 1)
                        dve.wait_ge(s_ch, t + 1)
                        chain(dve.tensor_tensor(self.weight[:, t, :], sc, chosen[:, t, :], ALU.mult))
                        chain(dve.tensor_reduce(wsum[:, t:t + 1], self.weight[:, t, :], AX, ALU.add))
                        chain(dve.reciprocal(wsum[:, t:t + 1], wsum[:, t:t + 1]))
                        chain(dve.tensor_scalar(self.weight[:, t, :], self.weight[:, t, :], wsum[:, t:t + 1], ROUTED_SCALE, ALU.mult, ALU.mult))
                    steps = -(-n * P // slots)
                    dve.wait_ge(s_rank, 1)
                    for i in range(steps):
                        ins = dve.tensor_scalar(more[:, i:i + 1], ps[0:NE, CB, 0:1], float(slots * i), None, ALU.is_gt)
                    chain(ins)
                    chain(dve.tensor_reduce(col[:], more[:, 0:steps], AX, ALU.add))
                    chain(dve.tensor_copy(count[:, 0:1], ps[0:NE, CB, 0:1]))
                    chain(dve.scalar_tensor_tensor(count[:, 1:2], col[:], float(-slots), count[:, 0:1], ALU.mult, ALU.add))
                    chain(dve.tensor_scalar(wide[:, 0, :], self.k("ones")[0:NE, :], count[:, 0:1], None, ALU.mult))
                    dve.tensor_scalar(wide[:, 1, :], self.k("ones")[0:NE, :], count[:, 1:2], None, ALU.mult).then_inc(s_wide, 1)
                    dve.wait_ge(s_cum, 1)
                    chain(dve.tensor_copy(more[:, 0:1], ps[0:NE, CB, 1:2]))
                    dve.tensor_scalar(begun[:], self.k("iota")[0:NE, 0:BLOCKS + 8], more[:, 0:1], None, ALU.is_ge).then_inc(s_beg, 1)
                    chain(dve.tensor_scalar(first[:], ps[:, CB, 64:64 + NE], 1.0, None, ALU.add))
                    chain(dve.tensor_copy(total[:, 0:1], ps[0:1, CB, 2:3]))
                    chain(dve.tensor_scalar(one[:, 0:BLOCKS // UNROLL], self.k("iota")[0:1, 0:BLOCKS // UNROLL], float(UNROLL), total[:, 0:1], ALU.mult, ALU.is_lt))
                    chain(dve.tensor_reduce(total[:, 1:2], one[:, 0:BLOCKS // UNROLL], AX, ALU.add))
                    chain(dve.tensor_scalar(self.turns[:], total[:, 1:2], -1.0, None, ALU.add))
                    dve.wait_ge(s_bx, 1)
                    chain(dve.tensor_scalar(self.block_expert[:], ps[0:1, XB, 0:BLOCKS + 8], float(NE - 1), None, ALU.min))
                    chain(dve.scalar_tensor_tensor(self.block_first[:], self.k("base"), float(slots), ps[:, XB, 128:128 + BLOCKS + 8], ALU.mult, ALU.add))
                    chain(dve.tensor_scalar(self.block_first[:], self.block_first[:], 1.0, None, ALU.add))
                    for t in range(n):
                        chain(dve.tensor_tensor(self.key[:, t, :], ps[:, RB, t * NE:(t + 1) * NE], first[:], ALU.add))
                        chain(dve.tensor_tensor(self.key[:, t, :], self.key[:, t, :], chosen[:, t, :], ALU.mult))
                        chain(dve.max(k8[:], self.key[:, t, :]))
                        keys = self.key[:, t:t + 1, :].broadcast_to((P, 8, NE))
                        mine = k8[:].rearrange("p (k a) -> p k a", a=1).broadcast_to((P, 8, NE))
                        chain(dve.tensor_tensor(hit[:], keys, mine, ALU.is_equal))
                        eight = self.k("iota")[:, 0:8].rearrange("p (k a) -> p k a", a=1).broadcast_to((P, 8, NE))
                        chain(dve.tensor_tensor(hit[:], hit[:], eight, ALU.mult))
                        chain(dve.tensor_reduce(self.place[:, t, :], hit[:].rearrange("p k e -> p e k"), AX, ALU.add))

    def expert_blocks(self, layer, n, size):
        nc, a, ps = self.nc, self.a, self.ps
        TOPB, IDB, GUB, HB, YB = 0, 2, 3, 4, 5
        words = KC * FF
        with ExitStack() as st:
            more = self.sb(st, "ring_more", [P, 2 * 3 * words])
            both = (self.ring[:].rearrange("p a n -> p (a n)"), more[:])
            quarter = [both[j // 2][:, (j % 2) * 3 * words:(j % 2 + 1) * 3 * words] for j in range(UNROLL)]
            gu = [q[:, 0:2 * words].rearrange("p (s c n) -> p c s n", s=2, c=KC) for q in quarter]
            dn = [q[:, 2 * words:].rearrange("p (c n) -> p c n", c=2) for q in quarter]
            at = self.sb(st, "slot_in_block", [P, 2, NT])
            pick = self.sb(st, "pick", [P, 2, NT, P], BF16)
            spot = self.sb(st, "spot", [P, 2, NT, 4], BF16)
            sums = self.sb(st, "spot_sums", [P, 2, 4])
            spots = self.sb(st, "row_of_slot", [P, 2])
            to_rows = self.sb(st, "to_rows", [P, BLOCKS + 8])
            from_row = self.sb(st, "from_row", [P, UNROLL], I32)
            to_row = self.sb(st, "to_row", [P, UNROLL], I32)
            x = self.sb(st, "x", [P, UNROLL, D])
            xT = self.sb(st, "x_T", [P, 2, KC, P])
            silu = self.sb(st, "silu", [P, FF])
            hid = self.sb(st, "hidden", [P, FF])
            hT = self.sb(st, "hidden_T", [P, 2, P])
            y = self.sb(st, "y", [P, UNROLL, D])
            primer = self.sb(st, "primer", [1, UNROLL, 8])
            k8 = self.sb(st, "key8", [P, 8])
            hit = self.sb(st, "hit", [P, 8, NE])
            held = self.sb(st, "held", [P, 8])
            s_gu = [self.sem(st, f"gate_up_loaded{j}") for j in range(UNROLL)]
            s_dn = [self.sem(st, f"down_loaded{j}") for j in range(UNROLL)]
            s_x = [self.sem(st, f"x_gathered{j}") for j in range(UNROLL)]
            s_st = [self.sem(st, f"y_scattered{j}") for j in range(UNROLL)]
            (s_x0, s_at, s_pick, s_id, s_sp, s_tok, s_turn, s_xv, s_xa, s_mm, s_silu, s_hid, s_tr, s_hT, s_dm, s_ya, s_hg, s_hs, s_to, s_w8) = (
                self.sem(st, q) for q in (
                    "x_cleared", "slots_ready", "picks_ready", "token_ids", "spots_chain", "rows_ready", "x_turned", "x_T_dve", "x_T_act",
                    "gate_up_done", "silu_done", "hidden_ready", "hidden_turned", "hidden_T_ready", "down_done", "y_copied",
                    "gather_wait_held", "scatter_wait_held", "to_row_ready", "weights_chain"))

            def turns_of(eng):
                return eng.value_load(self.turns[0:1, 0:1], min_val=TOPK // UNROLL - 1, max_val=BLOCKS // UNROLL - 1)

            def body(eng, turns, block_of):
                with eng.Fori(0, turns) as turn:
                    for j in range(UNROLL):
                        block_of(turn, j, UNROLL)
                for j in range(UNROLL):
                    block_of(turns, j, UNROLL - 1 - j)

            with nc.Block() as block:
                @block.sync
                def _(sp):
                    turns = turns_of(sp)

                    def load(turn, j, first):
                        b = j if first else UNROLL * turn + (UNROLL + j)
                        e = sp.value_load(self.block_expert[0:1, bass.ds(b, 1)], min_val=0, max_val=NE - 1)
                        if not first:
                            sp.wait_ge(s_mm, UNROLL * turn + (j + 1))
                        sp.dma_start(quarter[j][:, 0:words], a["exp_w_gate"][layer, bass.ds(e, 1)].rearrange("e (p c) n -> p (e c n)", c=KC)).then_inc(s_gu[j], 16)
                        sp.dma_start(quarter[j][:, words:2 * words], a["exp_w_up"][layer, bass.ds(e, 1)].rearrange("e (p c) n -> p (e c n)", c=KC)).then_inc(s_gu[j], 16)
                        if not first:
                            sp.wait_ge(s_dm, UNROLL * turn + (j + 1))
                        sp.dma_start(quarter[j][:, 2 * words:], a["exp_w_down"][layer, bass.ds(e, 1)].rearrange("e (p c) n -> p (e c n)", c=2)).then_inc(s_dn[j], 16)

                    for j in range(UNROLL):
                        if j:
                            sp.wait_ge(s_x[j - 1], 16)
                        load(0, j, True)
                    with sp.Fori(0, turns) as turn:
                        for j in range(UNROLL):
                            load(turn, j, False)

                @block.gpsimd
                def _(pool):
                    turns = turns_of(pool)

                    def hold(column, sem):
                        pool.tensor_tensor(held[:, column:column + 1], self.k("one"), self.k("one"), ALU.add).then_inc(sem, 1)

                    def gather(b, j):
                        pool.wait_ge(s_tok, b + 1)
                        if not isinstance(b, int):
                            hold(0, s_hg)
                        pool.indirect_dma_start(x[0:size, j, :], None, self.v_dram[0:n * P, :], bass.IndirectOffsetOnAxis(from_row[0:size, j:j + 1], 0),
                                                bounds_check=n * P - 1, oob_is_err=False).then_inc(s_x[j], 16)

                    def scatter(b, j):
                        pool.wait_ge(s_ya, 2 * b + 3)
                        hold(1, s_hs)
                        pool.indirect_dma_start(self.y_dram[0:n * P * TOPK, :], bass.IndirectOffsetOnAxis(to_row[0:size, j:j + 1], 0), y[0:size, j, :], None,
                                                bounds_check=n * P * TOPK - 1, oob_is_err=False).then_inc(s_st[j], 16)

                    for j in range(UNROLL):
                        pool.dma_start(primer[:, j, :], self.v_dram[0:1, 0:8]).then_inc(s_st[j], 16)
                    pool.memset(x[:], 0.0).then_inc(s_x0, 1)
                    hold(0, s_hg)
                    hold(1, s_hs)
                    pool.wait_ge(s_x0, 1)
                    for b in range(AHEAD):
                        gather(b, b % UNROLL)

                    def block_of(turn, j, ahead):
                        b = UNROLL * turn + j
                        if ahead >= UNROLL:
                            gather(b + AHEAD, (j + AHEAD) % UNROLL)
                        scatter(b, j)

                    body(pool, turns, block_of)
                    for j in range(UNROLL):
                        pool.wait_ge(s_st[j], 16 * turns + 32)
                        pool.tensor_tensor(held[:, 3 + j:4 + j], self.k("one"), self.k("one"), ALU.add)
                    pool.wait_ge(s_x[0], 16 * turns + 32)
                    pool.tensor_tensor(held[:, 2:3], self.k("one"), self.k("one"), ALU.add)

                @block.tensor
                def _(pe):
                    turns = turns_of(pe)

                    def ids(b, j):
                        pe.wait_ge(s_pick, b + 1)
                        for t in range(n):
                            mm = pe.matmul(ps[:, IDB, 0:4], pick[:, j % 2, t, :], spot[:, j % 2, t, :], start=(t == 0), stop=(t == n - 1))
                        mm.then_inc(s_id, 1)

                    def turn_x(b, j, turn):
                        pe.wait_ge(s_x[j], 16 * turn + 16)
                        if not isinstance(b, int) or b:
                            pe.wait_ge(s_xv, b)
                            pe.wait_ge(s_xa, b)
                        xs = x[:, j, :].rearrange("p (q c) -> p c q", c=KC)
                        for c in range(KC):
                            tr = pe.transpose(ps[:, TOPB + c // 4, (c % 4) * P:(c % 4 + 1) * P], xs[:, c, :], self.k("ident"))
                        tr.then_inc(s_turn, 1)

                    def gate_up(b, j, turn):
                        pe.wait_ge(s_gu[j], 32 * turn + 32)
                        pe.wait_ge(s_xv, b + 1)
                        pe.wait_ge(s_xa, b + 1)
                        for c in range(KC):
                            mm = pe.matmul(ps[:, GUB, :], xT[:, j % 2, c, :], gu[j][:, c, :, :], start=(c == 0), stop=(c == KC - 1))
                        mm.then_inc(s_mm, 1)

                    def turn_hidden(b):
                        pe.wait_ge(s_hid, b + 1)
                        h = hid[:].rearrange("p (q c) -> p c q", c=2)
                        for c in range(2):
                            tr = pe.transpose(ps[:, HB, c * P:(c + 1) * P], h[:, c, :], self.k("ident"))
                        tr.then_inc(s_tr, 1)

                    def down(b, j, turn):
                        pe.wait_ge(s_dn[j], 16 * turn + 16)
                        pe.wait_ge(s_hT, b + 1)
                        pe.wait_ge(s_ya, 2 * b + 1)
                        for half in range(2):
                            for c in range(2):
                                mm = pe.matmul(ps[:, YB + half, :], hT[:, c, :], dn[j][:, c, half * 512:(half + 1) * 512],
                                               start=(c == 0), stop=(c == 1))
                        mm.then_inc(s_dm, 1)

                    for b in range(UNROLL):
                        ids(b, b)
                    turn_x(0, 0, 0)
                    ids(UNROLL, 0)
                    gate_up(0, 0, 0)
                    turn_x(1, 1, 0)
                    turn_hidden(0)

                    def block_of(turn, j, ahead):
                        b = UNROLL * turn + j
                        if ahead >= UNROLL:
                            ids(b + AHEAD, (j + AHEAD) % UNROLL)
                        if ahead >= 1:
                            gate_up(b + 1, (j + 1) % UNROLL, turn + (j + 1) // UNROLL)
                        if ahead >= 2:
                            turn_x(b + 2, (j + 2) % UNROLL, turn + (j + 2) // UNROLL)
                        down(b, j, turn)
                        if ahead >= 1:
                            turn_hidden(b + 1)

                    body(pe, turns, block_of)

                @block.vector
                def _(dve):
                    turns = turns_of(dve)

                    def slots(b, j):
                        e = dve.value_load(self.block_expert[0:1, bass.ds(b, 1)], min_val=0, max_val=NE - 1)
                        base = self.block_first[:, bass.ds(b, 1)].broadcast_to((P, n))
                        dve.tensor_copy(spot[:, j % 2, 0:n, 3], self.place[:, 0:n, bass.ds(e, 1)].rearrange("p t e -> p (t e)"))
                        dve.tensor_tensor(at[:, j % 2, 0:n], self.key[:, 0:n, bass.ds(e, 1)].rearrange("p t e -> p (t e)"), base, ALU.subtract).then_inc(s_at, 1)
                        dve.wait_ge(s_at, b + 1)
                        for t in range(n):
                            ins = dve.tensor_scalar(pick[:, j % 2, t, :], self.k("iota"), at[:, j % 2, t:t + 1], None, ALU.is_equal)
                        ins.then_inc(s_pick, 1)

                    def rows(b, j):
                        dve.wait_ge(s_id, b + 1)
                        dve.tensor_tensor(sums[:], ps[:, IDB:IDB + 1, 0:4].broadcast_to((P, 2, 4)), self.k("spot_words").rearrange("p (r w) -> p r w", r=2), ALU.mult).then_inc(s_sp, 1)
                        dve.wait_ge(s_sp, 2 * b + 1)
                        dve.tensor_reduce(spots[:], sums[:], AX, ALU.add).then_inc(s_sp, 1)
                        dve.wait_ge(s_sp, 2 * b + 2)
                        dve.tensor_scalar(to_rows[:, bass.ds(b, 1)], spots[:, 1:2], FAR, None, ALU.add)
                        dve.tensor_scalar(from_row[:, j:j + 1], spots[:, 0:1], FAR, None, ALU.add).then_inc(s_tok, 1)

                    def x_half(b, j):
                        dve.wait_ge(s_turn, b + 1)
                        dve.tensor_copy(xT[:, j % 2, 0:4, :], ps[:, TOPB, :].rearrange("p (c t) -> p c t", c=4)).then_inc(s_xv, 1)

                    def hidden(b):
                        dve.wait_ge(s_silu, b + 1)
                        dve.tensor_tensor(hid[:], silu[:], ps[:, GUB, FF:], ALU.mult).then_inc(s_hid, 1)

                    def hidden_T(b):
                        dve.wait_ge(s_tr, b + 1)
                        dve.tensor_copy(hT[:], ps[:, HB, 0:2 * P].rearrange("p (c t) -> p c t", c=2)).then_inc(s_hT, 1)

                    for half in range(2):
                        dve.tensor_copy(spot[:, half, 0:NT, 0:3], self.k("spot").rearrange("p (t w) -> p t w", w=3))
                    for b in range(UNROLL):
                        slots(b, b)
                        rows(b, b)
                    slots(UNROLL, 0)
                    x_half(0, 0)
                    rows(UNROLL, 0)
                    slots(AHEAD, 1)
                    hidden(0)
                    x_half(1, 1)
                    hidden_T(0)
                    chain = Chain(dve, s_w8)
                    for t in range(n):
                        chain(dve.max(k8[:], self.key[:, t, :]))
                        keys = self.key[:, t:t + 1, :].broadcast_to((P, 8, NE))
                        mine = k8[:].rearrange("p (k a) -> p k a", a=1).broadcast_to((P, 8, NE))
                        chain(dve.tensor_tensor(hit[:], keys, mine, ALU.is_equal))
                        chain(dve.tensor_tensor(hit[:], hit[:], self.weight[:, t:t + 1, :].broadcast_to((P, 8, NE)), ALU.mult))
                        chain(dve.tensor_reduce(self.w8[:, t, :], hit[:], AX, ALU.add))

                    def block_of(turn, j, ahead):
                        b = UNROLL * turn + j
                        if ahead >= UNROLL:
                            dve.wait_ge(s_hg, b + 1)
                            rows(b + AHEAD, (j + AHEAD) % UNROLL)
                        dve.wait_ge(s_st[j], 16 * turn + 16)
                        dve.tensor_scalar(to_row[:, j:j + 1], to_rows[:, bass.ds(b, 1)], 0.0, None, ALU.add).then_inc(s_to, 1)
                        if ahead >= UNROLL:
                            slots(b + AHEAD + 1, (j + AHEAD + 1) % UNROLL)
                        if ahead >= 1:
                            hidden(b + 1)
                        if ahead >= 2:
                            x_half(b + 2, (j + 2) % UNROLL)
                        if ahead >= 1:
                            hidden_T(b + 1)

                    body(dve, turns, block_of)

                @block.scalar
                def _(act):
                    turns = turns_of(act)

                    def x_half(b, j):
                        act.wait_ge(s_turn, b + 1)
                        act.activation(xT[:, j % 2, 4:8, :], ps[:, TOPB + 1, :].rearrange("p (c t) -> p c t", c=4), ACT.Copy).then_inc(s_xa, 1)

                    def gate(b):
                        act.wait_ge(s_mm, b + 1)
                        act.activation(silu[:], ps[:, GUB, 0:FF], ACT.Silu).then_inc(s_silu, 1)

                    act.sem_inc(s_ya, 1)
                    x_half(0, 0)
                    gate(0)
                    x_half(1, 1)

                    def block_of(turn, j, ahead):
                        b = UNROLL * turn + j
                        if ahead >= 1:
                            gate(b + 1)
                        if ahead >= 2:
                            x_half(b + 2, (j + 2) % UNROLL)
                        act.wait_ge(s_st[j], 16 * turn + 16)
                        act.wait_ge(s_hs, b + 1)
                        act.wait_ge(s_to, b + 1)
                        act.wait_ge(s_dm, b + 1)
                        for half in range(2):
                            ins = act.activation(y[:, j, half * 512:(half + 1) * 512], ps[:, YB + half, :], ACT.Copy)
                            ins.then_inc(s_ya, 1)

                    body(act, turns, block_of)

    def combine(self, layer, n, f, vT):
        nc, a, ps = self.nc, self.a, self.ps
        R, PER = 3, 4
        with ExitStack() as st:
            rows = self.sb(st, "expert_rows", [P, R, PER, D])
            silu = self.sb(st, "silu", [P, 2, FF])
            hid = self.sb(st, "hidden", [P, 2, FF])
            hT = self.sb(st, "hidden_T", [P, 2, 2, P])
            s_row = [self.sem(st, f"rows_loaded{i}") for i in range(R)]
            s_gu, s_dn = self.sem(st, "gate_up_loaded"), self.sem(st, "down_loaded")
            s_add, s_mm, s_silu, s_hid, s_tr, s_hT, s_y, s_f = (self.sem(st, x) for x in (
                "row_added", "gate_up_done", "silu_done", "hidden_ready", "hidden_turned", "hidden_T_ready", "down_done", "shared_added"))
            gu = self.sb(st, "shared_gate_up", [P, KC, 2, FF])
            dn = self.sb(st, "shared_down", [P, 2, D])
            chunks = n * TOPK // PER
            with nc.Block() as block:
                @block.sync
                def _(sp):
                    for s, name in enumerate(("sh_w_gate", "sh_w_up")):
                        sp.dma_start(gu[:, :, s, :], a[name][layer].rearrange("(p c) n -> p c n", c=KC)).then_inc(s_gu, 16)
                    sp.dma_start(dn[:], a["sh_w_down"][layer].rearrange("(p c) n -> p c n", c=2)).then_inc(s_dn, 16)
                    yv = self.y_dram.rearrange("(t p k) d -> t p k d", p=P, k=TOPK)
                    for i in range(chunks):
                        t, half = divmod(i, TOPK // PER)
                        if i >= R:
                            sp.wait_ge(s_add, PER * (i - R + 1))
                        sp.dma_start(rows[:, i % R, :, :], yv[t, :, half * PER:(half + 1) * PER, :]).then_inc(s_row[i % R], 16)
                    self.stream.load(sp, self.behind)

                @block.tensor
                def _(pe):
                    def gate_up(t):
                        if t >= 2:
                            pe.wait_ge(s_hid, t - 1)
                        for c in range(KC):
                            mm = pe.matmul(ps[:, t % 2, :], vT[:, c, t * P:(t + 1) * P], gu[:, c, :, :], start=(c == 0), stop=(c == KC - 1))
                        mm.then_inc(s_mm, 1)

                    def down(t):
                        pe.wait_ge(s_hid, t + 1)
                        if t >= 2:
                            pe.wait_ge(s_hT, t - 1)
                        h = hid[:, t % 2, :].rearrange("p (q c) -> p c q", c=2)
                        for c in range(2):
                            tr = pe.transpose(ps[:, 2 + t % 2, c * P:(c + 1) * P], h[:, c, :], self.k("ident"))
                        tr.then_inc(s_tr, 1)
                        pe.wait_ge(s_hT, t + 1)
                        if t >= 2:
                            pe.wait_ge(s_f, 2 * (t - 1))
                        for half in range(2):
                            for c in range(2):
                                mm = pe.matmul(ps[:, 4 + 2 * (t % 2) + half, :], hT[:, t % 2, c, :], dn[:, c, half * 512:(half + 1) * 512],
                                               start=(c == 0), stop=(c == 1))
                        mm.then_inc(s_y, 1)

                    pe.wait_ge(s_gu, 32)
                    for t in range(n):
                        gate_up(t)
                        if t == 1:
                            pe.wait_ge(s_dn, 16)
                        if t:
                            down(t - 1)
                    down(n - 1)

                @block.scalar
                def _(act):
                    def turned(t):
                        act.wait_ge(s_tr, t + 1)
                        act.activation(hT[:, t % 2, :, :], ps[:, 2 + t % 2, 0:2 * P].rearrange("p (c t) -> p c t", c=2), ACT.Copy).then_inc(s_hT, 1)

                    for t in range(n):
                        act.wait_ge(s_mm, t + 1)
                        if t >= 2:
                            act.wait_ge(s_hid, t - 1)
                        act.activation(silu[:, t % 2, :], ps[:, t % 2, 0:FF], ACT.Silu).then_inc(s_silu, 1)
                        if t:
                            turned(t - 1)
                    turned(n - 1)

                @block.vector
                def _(dve):
                    def hidden(t):
                        dve.wait_ge(s_silu, t + 1)
                        if t >= 2:
                            dve.wait_ge(s_tr, t - 1)
                        dve.tensor_tensor(hid[:, t % 2, :], silu[:, t % 2, :], ps[:, t % 2, FF:], ALU.mult).then_inc(s_hid, 1)

                    def add_rows(i):
                        t, half = divmod(i, TOPK // PER)
                        dve.wait_ge(s_row[i % R], 16 * (i // R + 1))
                        for k in range(PER):
                            w = self.w8[:, t, half * PER + k:half * PER + k + 1]
                            if half == 0 and k == 0:
                                dve.tensor_scalar(f[:, t, :], rows[:, i % R, k, :], w, None, ALU.mult).then_inc(s_add, 1)
                            else:
                                dve.scalar_tensor_tensor(f[:, t, :], rows[:, i % R, k, :], w, f[:, t, :], ALU.mult, ALU.add).then_inc(s_add, 1)
                            dve.wait_ge(s_add, PER * i + k + 1)

                    def add_shared(t):
                        dve.wait_ge(s_y, t + 1)
                        for half in range(2):
                            cols = slice(half * 512, (half + 1) * 512)
                            dve.tensor_tensor(f[:, t, cols], f[:, t, cols], ps[:, 4 + 2 * (t % 2) + half, :], ALU.add).then_inc(s_f, 1)

                    add_rows(0)
                    add_rows(1)
                    hidden(0)
                    for t in range(1, n):
                        add_rows(2 * t)
                        hidden(t)
                        add_rows(2 * t + 1)
                        add_shared(t - 1)
                    add_shared(n - 1)
                    dve.wait_ge(s_f, 2 * n)

    def layer1(self):
        a, tiles, lat = self.a, list(range(NT)), list(range(NL))
        with ExitStack() as st:
            mixed = self.sb(st, "mixed", [P, NL, D])
            with ExitStack() as s1:
                z = self.sb(s1, "z", [P, NL, SI])
                dq = self.sb(s1, "dq", [P, NL, 2 * DH * DD])
                dk = self.sb(s1, "dk", [P, NT, 2 * DH * DD])
                dv = self.sb(s1, "dv", [P, NT, DH * DV])
                dt = self.sb(s1, "dt", [P, NT, 2 * SH])
                xbcT = self.sb(s1, "xbc_T", [P, XBC // P, NT * P])
                with ExitStack() as s2:
                    u = self.sb(s2, "u", [P, NT, D])
                    uT = self.sb(s2, "uT", [P, KC, NT * P])
                    jobs = [(R_XBC + n, 512, [(None, xbcT[:, n // P + i, :]) for i in range(4)]) for n in range(0, XBC, 512)]
                    jobs += [(R_DT, 2 * SH, [(t, dt[:, t, :]) for t in tiles]),
                             (R_DK, 512, [(t, dk[:, t, :]) for t in tiles]),
                             (R_DV, 512, [(t, dv[:, t, :]) for t in tiles]),
                             (R_DQ, 512, [(t, dq[:, t, :]) for t in lat]),
                             (0, 512, [(t, z[:, t, :]) for t in lat])]
                    planned = self.plan(a["rec_w_in"][0], KC, jobs)
                    self.norm_modulate(1, False, tiles, u, uT)
                    diff_rows = self.modulation(19, 2)
                    self.linear(planned, uT)
                self.diff_attention(dq, dk, dv, mixed, diff_rows)
                w_out = self.ssd(z, dt, xbcT, mixed)
            with ExitStack() as s1:
                mT = self.sb(s1, "mixed_T", [P, KC, NL * P])
                self.transpose_rows(lambda t: mixed[:, t, :], KC, lat, mT)
                self.linear(w_out, mT)
            self.residual(1, False, lat, mixed)
        if self.stop("mix1"):
            self.store_h()
            return
        self.clear_semaphores()
        self.experts(1, lat, 96)
        self.store_h()

    def diff_attention(self, dq, dk, dv, mixed, rows):
        nc, a = self.nc, self.a
        init = 0.8 - 0.6 * math.exp(-0.3)
        HD = 2 * DH
        with ExitStack() as st:
            lam = self.sb(st, "lambda_rows", [P, 4, DD])
            dots = self.sb(st, "lambda_dots", [P, 2])
            self.neg_lambda = self.sb(st, "neg_lambda", [P, 1])
            sub = self.sb(st, "subln", [P, DV])
            tmp = self.sb(st, "swapped", [P, HD * DD])
            qz = self.sb(st, "queries_padded", [P, NL, DH, 3 * DD])
            qT = self.sb(st, "qT", [2 * DD, HD, NL * P])
            kT = self.sb(st, "kT", [2 * DD, DH, NT * P])
            o = self.sb(st, "o", [P, NL, DH, DV])
            s_in, s_c, s_dot, s_e, s_z = (self.sem(st, x) for x in ("rows_loaded", "dve_chain", "dots_ready", "exp_done", "zeros_written"))
            with nc.Block() as block:
                self.rows_alone(block, rows)

                @block.sync
                def _(sp):
                    for i, name in enumerate(("diff_lambda_q1", "diff_lambda_k1", "diff_lambda_q2", "diff_lambda_k2")):
                        sp.dma_start(lam[:, i, :], bcast_rows(a[name][0], P)).then_inc(s_in, 16)
                    sp.dma_start(sub[:], bcast_rows(a["diff_subln"][0], P)).then_inc(s_in, 16)
                    self.beside_sp(sp, rows)

                @block.scalar
                def _(act):
                    act.wait_ge(s_dot, 1)
                    act.activation(dots[:], dots[:], ACT.Exp).then_inc(s_e, 1)
                    for i in range(rows.count):
                        rows.copy_out(act, i)

                @block.vector
                def _(dve):
                    chain = Chain(dve, s_c)
                    dve.memset(qz[:], 0.0).then_inc(s_z, 1)
                    dve.wait_ge(s_in, 80)
                    chain(dve.tensor_tensor(lam[:, 0:3:2, :], lam[:, 0:3:2, :], lam[:, 1:4:2, :], ALU.mult))
                    dve.tensor_reduce(dots[:], lam[:, 0:3:2, :], AX, ALU.add).then_inc(s_dot, 1)
                    for t in range(NL):
                        for x in (dq, dk):
                            chain(self.rope(chain, dve, x[:, t, :].rearrange("p (h d) -> p h d", d=DD), tmp, DD, t))
                    dve.wait_ge(s_z, 1)
                    heads = dq[:].rearrange("p t (h m d) -> p t h m d", m=2, d=DD)
                    for m in range(2):
                        chain(dve.tensor_copy(qz[:, :, :, 2 * m * DD:(2 * m + 1) * DD], heads[:, :, :, m, :]))
                    dve.wait_ge(s_e, 1)
                    chain(dve.tensor_scalar(dots[:, 0:1], dots[:, 0:1], init, None, ALU.add))
                    chain(dve.tensor_tensor(self.neg_lambda[:], dots[:, 1:2], dots[:, 0:1], ALU.subtract))
                    chain(dve.tensor_scalar(sub[:], sub[:], 1.0 - init, None, ALU.mult))
            self.conv_rows = self.modulation(21, 3)
            jobs = [(kT[:, h, :], [dk[:, t, 2 * h * DD:2 * (h + 1) * DD] for t in range(NT)], 1.0) for h in range(DH)]
            jobs += [(qT[:, i, :], [qz[:, t, i // 2, (i % 2) * DD:(i % 2 + 2) * DD] for t in range(NL)], DD ** -0.5) for i in range(HD)]
            self.transposed(jobs)
            items, outs = [], []
            for h in range(DH):
                for t in range(NL):
                    items.append({"q": [qT[:, 2 * h + m, t * P:(t + 1) * P] for m in range(2)],
                                  "k": [kT[:, h, :] for m in range(2)],
                                  "v": [dv[:, s, h * DV:(h + 1) * DV] for s in range(NT)]})
                    outs.append(o[:, t, h, :])
            self.attention(items, lambda i: outs[i])
            self.grouped_norm(o, DH, DV, [sub[:] for _ in range(DH)], lambda t, g: mixed[:, t, SI + g * DV:SI + (g + 1) * DV])

    def grouped_norm(self, x, groups, size, gains, dst):
        nc = self.nc
        with ExitStack() as st:
            junk = self.sb(st, "squares", [P, size])
            ss = self.sb(st, "ss", [P, NL * groups])
            s_a, s_r, s_d = (self.sem(st, q) for q in ("act_chain", "r_ready", "normed"))
            pairs = [(t, g) for t in range(NL) for g in range(groups)]
            with nc.Block() as block:
                @block.scalar
                def _(act):
                    act.preload_act_table_set("natural_log_exp_and_others")
                    chain = Chain(act, s_a)
                    for i, (t, g) in enumerate(pairs):
                        chain(act.activation(junk[:], x[:, t, g, :], ACT.Square, accum_out=ss[:, i:i + 1]))
                    chain(act.activation(ss[:], ss[:], ACT.Ln, scale=1.0 / size, bias=self.k("eps")))
                    act.activation(ss[:], ss[:], ACT.Exp, scale=-0.5).then_inc(s_r, 1)

                @block.vector
                def _(dve):
                    dve.wait_ge(s_r, 1)
                    for i, (t, g) in enumerate(pairs):
                        dve.scalar_tensor_tensor(dst(t, g), x[:, t, g, :], ss[:, i:i + 1], gains[g], ALU.mult, ALU.mult).then_inc(s_d, 1)
                    dve.wait_ge(s_d, len(pairs))

    def ssd(self, z, dt, xbcT, mixed):
        nc, a, ps = self.nc, self.a, self.ps
        rows = self.conv_rows
        w_out = self.plan(a["mix_w_out"][1], KC, [(n, 512, [(t, mixed[:, t, n:n + 512]) for t in range(NL)]) for n in (0, 512)])
        CH = XBC // P
        with ExitStack() as st:
            conv = self.sb(st, "conv", [P, CH, NT * P])
            xs = self.sb(st, "xs", [P, NT, SH, SP_])
            bm = self.sb(st, "bm", [P, NT, SG * SN])
            adt = self.sb(st, "a_dt", [P, NT, 2 * SH])
            y = self.sb(st, "y", [P, NL, SG, SI // SG])
            skip = self.sb(st, "skip", [P, SH])
            gain = self.sb(st, "ssd_gain", [P, SI])
            with ExitStack() as s1:
                cw = self.sb(s1, "conv_w", [P, CH, 3])
                cb = self.sb(s1, "conv_b", [P, CH])
                dtb = self.sb(s1, "dt_bias", [P, 2 * SH])
                al = self.sb(s1, "a_log", [P, 2 * SH])
                pos = self.sb(s1, "dt_positive", [P, NT, 2 * SH])
                s_cw, s_in, s_c, s_cv, s_dt, s_e, s_si = (self.sem(s1, q) for q in (
                    "conv_w_loaded", "rows_loaded", "dve_chain", "convolved", "dt_absolute", "exp_done", "silu_done"))
                with nc.Block() as block:
                    self.rows_alone(block, rows)

                    @block.sync
                    def _(sp):
                        with nc.allow_non_contiguous_dma("3072 words of filter"):
                            for i in range(3):
                                sp.dma_start(cw[:, :, i], a["ssd_conv_w"][0, i].rearrange("(m p) -> p m", p=P)).then_inc(s_cw, 16)
                            sp.dma_start(cb[:], a["ssd_conv_b"][0].rearrange("(m p) -> p m", p=P)).then_inc(s_cw, 16)
                        for i, d in enumerate("fb"):
                            sp.dma_start(dtb[:, i * SH:(i + 1) * SH], bcast_rows(a[f"ssd_dt_bias_{d}"][0], P)).then_inc(s_in, 16)
                            sp.dma_start(al[:, i * SH:(i + 1) * SH], bcast_rows(a[f"ssd_a_log_{d}"][0], P)).then_inc(s_in, 16)
                        sp.dma_start(skip[:], bcast_rows(a["ssd_d"][0], P)).then_inc(s_in, 16)
                        sp.dma_start(gain[:], bcast_rows(a["ssd_norm"][0], P)).then_inc(s_in, 16)
                        self.beside_sp(sp, rows)

                    @block.scalar
                    def _(act):
                        chain = Chain(act, s_e)
                        act.wait_ge(s_in, 96)
                        chain(act.activation(al[:], al[:], ACT.Exp))
                        act.wait_ge(s_dt, 1)
                        chain(act.activation(adt[:], adt[:], ACT.Exp, scale=-1.0))
                        chain(act.activation(adt[:], adt[:], ACT.Ln, bias=self.k("one")))
                        for m in range(CH):
                            act.wait_ge(s_cv, m + 1)
                            act.activation(conv[:, m, :], conv[:, m, :], ACT.Silu).then_inc(s_si, 1)
                        for i in range(rows.count):
                            rows.copy_out(act, i)

                    @block.vector
                    def _(dve):
                        chain = Chain(dve, s_c)
                        dve.wait_ge(s_in, 96)
                        chain(dve.tensor_tensor(dt[:], dt[:], dtb[:].rearrange("p (a h) -> p a h", a=1).broadcast_to((P, NT, 2 * SH)), ALU.add))
                        chain(dve.tensor_scalar(pos[:], dt[:], 0.0, None, ALU.max))
                        dve.scalar_tensor_tensor(adt[:], dt[:], -1.0, dt[:], ALU.mult, ALU.max).then_inc(s_dt, 1)
                        dve.wait_ge(s_cw, 64)
                        for m in range(CH):
                            x, o = xbcT[:, m, :], conv[:, m, :]
                            chain(dve.tensor_scalar(o, x, cw[:, m, 1:2], cb[:, m:m + 1], ALU.mult, ALU.add))
                            xg = x.rearrange("p (s t) -> p s t", s=2)
                            og = o.rearrange("p (s t) -> p s t", s=2)
                            chain(dve.scalar_tensor_tensor(og[:, :, 1:], xg[:, :, 0:SEQ - 1], cw[:, m, 0:1], og[:, :, 1:], ALU.mult, ALU.add))
                            dve.scalar_tensor_tensor(og[:, :, 0:SEQ - 1], xg[:, :, 1:], cw[:, m, 2:3], og[:, :, 0:SEQ - 1], ALU.mult, ALU.add).then_inc(s_cv, 1)
                            if m == 0:
                                dve.wait_ge(s_e, 3)
                                chain(dve.tensor_tensor(dt[:], pos[:], adt[:], ALU.add))
                                alb = al[:].rearrange("p (a h) -> p a h", a=1).broadcast_to((P, NT, 2 * SH))
                                chain(dve.scalar_tensor_tensor(adt[:], dt[:], -1.0, alb, ALU.mult, ALU.mult))
            jobs = []
            for t in range(NT):
                cols = slice(t * P, (t + 1) * P)
                jobs.append((xs[:, t, :, :].rearrange("p (c a) d -> p c (a d)", a=2), [conv[:, m, cols] for m in range(4)], 1.0))
                jobs.append((bm[:, t, :].rearrange("p (c d) -> p c d", c=2), [conv[:, m, cols] for m in (4, 5)], 1.0))
            self.transposed(jobs)
            self.ssd_scan(conv, xs, bm, dt, adt, y)
            with ExitStack() as s1:
                s_c, s_z, s_y = (self.sem(s1, q) for q in ("dve_chain", "silu_z", "y_gated"))
                tmp = self.sb(s1, "skipped", [P, SH, SP_])
                with nc.Block() as block:
                    @block.scalar
                    def _(act):
                        act.activation(z[:], z[:], ACT.Silu).then_inc(s_z, 1)

                    @block.vector
                    def _(dve):
                        chain = Chain(dve, s_c)
                        dve.wait_ge(s_z, 1)
                        for t in range(NL):
                            yt = y[:, t, :, :].rearrange("p g n -> p (g n)")
                            skips = skip[:].rearrange("p (h a) -> p h a", a=1).broadcast_to((P, SH, SP_))
                            chain(dve.tensor_tensor(tmp[:], xs[:, t, :, :], skips, ALU.mult))
                            chain(dve.tensor_tensor(yt, yt, tmp[:].rearrange("p h d -> p (h d)"), ALU.add))
                            chain(dve.tensor_tensor(yt, yt, z[:, t, :], ALU.mult))
            W = SI // SG
            self.grouped_norm(y, SG, W, [gain[:, g * W:(g + 1) * W] for g in range(SG)], lambda t, g: mixed[:, t, g * W:(g + 1) * W])
        return w_out

    def ssd_scan(self, conv, xs, bm, dt, adt, y):
        nc, ps = self.nc, self.ps
        HG, W = SH // SG, SI // SG
        order = ([2, 3, 0, 1], [3, 2, 1, 0])
        steps = [(d, order[d][i], i) for i in range(NT) for d in range(2)]
        with ExitStack() as st:
            state = self.sb(st, "state", [P, 2, SH, SP_])
            xd = self.sb(st, "x_dt", [P, SH, SP_])
            xe = self.sb(st, "x_dt_decayed", [P, SH, SP_])
            sums = self.sb(st, "decay_sums", [P, 3 * SH])
            ex = self.sb(st, "decays", [P, 3 * SH])
            wide = self.sb(st, "a_dt_wide", [P, SH, P])
            seg = self.sb(st, "segments", [P, SH, P])
            cbm = self.sb(st, "cb_masked", [P, SG, P])
            yo = self.sb(st, "y_chunk", [P, SH, SP_])
            s_c, s_w, s_1, s_sum, s_ex, s_seg, s_sx, s_G, s_2, s_xe, s_3, s_st = (self.sem(st, q) for q in (
                "dve_chain", "a_dt_wide_ready", "sums_done", "sums_copied", "decays_ready", "segments_ready", "segments_exp",
                "G_ready", "y_done", "x_decayed_ready", "state_added", "state_ready"))
            ys = [i for i, (d, t, n) in enumerate(steps) if n >= 2]
            zs = [i for i, (d, t, n) in enumerate(steps) if n < NT - 1]
            with nc.Block() as block:
                @block.tensor
                def _(pe):
                    for i, (d, t, n) in enumerate(steps):
                        tri = self.k("tri_le" if d == 0 else "tri_ge")
                        ad = adt[:, t, d * SH:(d + 1) * SH]
                        if i:
                            pe.wait_ge(s_st, i)
                        mm = pe.matmul(ps[:, 0, 0:SH], tri, ad, start=True, stop=True)
                        mm = pe.matmul(ps[:, 0, SH:2 * SH], self.k("ones"), ad, start=True, stop=True)
                        if n >= 2:
                            for g in range(SG):
                                pe.matmul(ps[:, 1, g * P:(g + 1) * P], conv[:, 4 + g, t * P:(t + 1) * P], conv[:, 6 + g, t * P:(t + 1) * P], start=True, stop=True)
                            pe.wait_ge(s_w, ys.index(i) + 1)
                            for h in range(SH):
                                mm = pe.matmul(ps[:, 2 + h // HG, (h % HG) * P:(h % HG + 1) * P], wide[:, h, :], tri, start=True, stop=True)
                        mm.then_inc(s_1, 1)
                        if n >= 2:
                            for g in range(SG):
                                pe.matmul(ps[:, 5, g * W:(g + 1) * W], conv[:, 6 + g, t * P:(t + 1) * P],
                                          state[:, d, g * HG:(g + 1) * HG, :], start=True, stop=True)
                            pe.wait_ge(s_G, ys.index(i) + 1)
                            for h in range(SH):
                                mm = pe.matmul(ps[:, 4, h * SP_:(h + 1) * SP_], seg[:, h, :], xd[:, h, :], start=True, stop=True)
                            mm.then_inc(s_2, 1)
                        if n < NT - 1:
                            pe.wait_ge(s_xe, zs.index(i) + 1)
                            for g in range(SG):
                                mm = pe.matmul(ps[:, 6, g * W:(g + 1) * W], bm[:, t, g * SN:(g + 1) * SN], xe[:, g * HG:(g + 1) * HG, :], start=True, stop=True)
                            mm.then_inc(s_3, 1)

                @block.scalar
                def _(act):
                    for i, (d, t, n) in enumerate(steps):
                        act.wait_ge(s_sum, i + 1)
                        act.activation(ex[:], sums[:], ACT.Exp).then_inc(s_ex, 1)
                        if n >= 2:
                            act.wait_ge(s_seg, ys.index(i) + 1)
                            act.activation(seg[:], seg[:], ACT.Exp).then_inc(s_sx, 1)

                @block.vector
                def _(dve):
                    chain = Chain(dve, s_c)

                    def per_head(x, width=SP_):
                        return x.rearrange("p (h a) -> p h a", a=1).broadcast_to((P, SH, width))

                    for i, (d, t, n) in enumerate(steps):
                        heads = slice(d * SH, (d + 1) * SH)
                        if n >= 2:
                            dve.tensor_copy(wide[:], per_head(adt[:, t, heads], P)).then_inc(s_w, 1)
                        chain(dve.tensor_tensor(xd[:], xs[:, t, :, :], per_head(dt[:, t, heads]), ALU.mult))
                        dve.wait_ge(s_1, i + 1)
                        chain(dve.tensor_copy(sums[:, 2 * SH:], ps[:, 0, 0:SH]))
                        chain(dve.tensor_copy(sums[:, SH:2 * SH], ps[:, 0, SH:2 * SH]))
                        dve.tensor_tensor(sums[:, 0:SH], sums[:, SH:2 * SH], sums[:, 2 * SH:], ALU.subtract).then_inc(s_sum, 1)
                        if n >= 2:
                            for h in range(SH):
                                ins = dve.tensor_scalar(seg[:, h, :], ps[:, 2 + h // HG, (h % HG) * P:(h % HG + 1) * P],
                                                        sums[:, 2 * SH + h:2 * SH + h + 1], 0.0, ALU.subtract, ALU.min)
                            ins.then_inc(s_seg, 1)
                            mask = self.k("tri_le" if d == 0 else "tri_ge").rearrange("p (a l) -> p a l", a=1).broadcast_to((P, SG, P))
                            chain(dve.tensor_tensor(cbm[:], ps[:, 1, 0:SG * P].rearrange("p (g l) -> p g l", g=SG), mask, ALU.mult))
                            dve.wait_ge(s_sx, ys.index(i) + 1)
                            for g in range(SG):
                                sg = seg[:, g * HG:(g + 1) * HG, :]
                                ins = dve.tensor_tensor(sg, sg, cbm[:, g:g + 1, :].broadcast_to((P, HG, P)), ALU.mult)
                            ins.then_inc(s_G, 1)
                        dve.wait_ge(s_ex, i + 1)
                        if n < NT - 1:
                            dve.tensor_tensor(xe[:], xd[:], per_head(ex[:, 0:SH]), ALU.mult).then_inc(s_xe, 1)
                        if n >= 2:
                            yt = y[:, t, :, :].rearrange("p g n -> p (g n)").rearrange("p (h d) -> p h d", h=SH)
                            dve.wait_ge(s_2, ys.index(i) + 1)
                            chain(dve.tensor_tensor(yo[:], ps[:, 5, :].rearrange("p (h d) -> p h d", h=SH), per_head(ex[:, 2 * SH:]), ALU.mult))
                            first = all(q[1] != t or q[2] < 2 for q in steps[:i])
                            if not first:
                                chain(dve.tensor_tensor(yt, yt, yo[:], ALU.add))
                            base = yo[:] if first else yt
                            ins = dve.tensor_tensor(yt, base, ps[:, 4, :].rearrange("p (h d) -> p h d", h=SH), ALU.add)
                            if n < NT - 1:
                                chain(ins)
                            else:
                                ins.then_inc(s_st, 1)
                        sd = state[:, d, :, :]
                        if n < NT - 1:
                            dve.wait_ge(s_3, zs.index(i) + 1)
                            new = ps[:, 6, :].rearrange("p (h d) -> p h d", h=SH)
                            if n == 0:
                                dve.tensor_copy(sd, new).then_inc(s_st, 1)
                            else:
                                chain(dve.tensor_tensor(sd, sd, per_head(ex[:, SH:2 * SH]), ALU.mult))
                                dve.tensor_tensor(sd, sd, new, ALU.add).then_inc(s_st, 1)
                        dve.wait_ge(s_st, i + 1)

    def store_h(self):
        nc = self.nc
        with ExitStack() as st:
            s_o = self.sem(st, "h_stored")
            with nc.Block() as block:
                @block.sync
                def _(sp):
                    for n in range(Modulation.SLOTS):
                        sp.wait_ge(self.s_rows_stored[n], 16 * (2 * Modulation.CHUNKS // Modulation.SLOTS))
                    for t in range(NL):
                        sp.dma_start(self.out[0, t * P:(t + 1) * P, :], self.h[:, t, :]).then_inc(s_o, 16)
                    sp.wait_ge(s_o, 16 * NL)


def kernel(**inputs):
    import concourse.bacc as bacc
    from concourse.bass_utils import run_bass_kernel_spmd as run

    nc = bacc.Bacc("TRN2", target_bir_lowering=False, num_devices=1)
    arrays = {name: np.ascontiguousarray(v) for name, v in inputs.items()}
    arrays["const"] = const_table()
    aps = {name: nc.dram_tensor(f"in_{name}", v.shape, mybir.dt.from_np(v.dtype), kind="ExternalInput").ap()
           for name, v in arrays.items()}
    out = nc.dram_tensor("out_h", (1, SEQ, D), F32, kind="ExternalOutput").ap()
    Net(nc, aps, out).build()
    r = run(nc, [{f"in_{name}": v for name, v in arrays.items()}], core_ids=[0])
    return r.results[0]["out_h"]
```
